# Optimizing a Trainium2 kernel written in Bass

```python
import jax, jax.numpy as jnp
from jax import lax
import numpy as np

D_MODEL = 1024
BATCH = 1
SEQ = 128
DEPTH = 2
DEC_BATCH = 1
DEC_SEQ = 512
PAST_LEN = 128

GRID_W = 64
HEAD_DIM = 64
A_HEADS = 8
A_KV_HEADS = 2
WINDOW = 128
ATTN_BLOCK = 128
B_HEADS = 4
CONV_W = 5
GDN_CHUNK = 64
C_HEADS = 4
HGRN_CHUNK = 64
D_A = A_HEADS * HEAD_DIM
D_KV = A_KV_HEADS * HEAD_DIM
D_B = B_HEADS * HEAD_DIM
D_C = C_HEADS * HEAD_DIM
D_MIX = D_A + D_B + D_C
D_IN = (D_A + 2 * D_KV) + (4 * D_B + 4 * B_HEADS) + 5 * D_C
D_FF = 2816
N_EXPERTS = 8
TOP_K = 2
EXPERT_FF = 1024
ROPE_THETA = 10000.0
NORM_EPS = 1e-5
MASK_VALUE = -1e30
TINY = 1e-30
F32 = jnp.float32

kernel_name = 'hybrid_flow_backbone_step'

def layer_norm(x, g, b):
    xf = x.astype(F32)
    mu = jnp.mean(xf, -1, keepdims=True)
    var = jnp.mean(jnp.square(xf - mu), -1, keepdims=True)
    return ((xf - mu) * lax.rsqrt(var + NORM_EPS) * g.astype(F32) + b.astype(F32)).astype(x.dtype)

def l2_normalize(x):
    return x * lax.rsqrt(jnp.sum(x * x, -1, keepdims=True) + 1e-6)

def gated_rms_readout(o, g, w):
    o = o * lax.rsqrt(jnp.mean(o * o, -1, keepdims=True) + NORM_EPS) * w.astype(F32)
    o = o * jax.nn.silu(g.astype(F32))
    return o.reshape(o.shape[0], o.shape[1], -1)

def modulation(cvec, w_mod, b_mod):
    m = jax.nn.silu(cvec) @ w_mod + b_mod
    return jnp.split(m[..., None, :], 6, axis=-1)

def rope_2d(x):
    T = x.shape[1]
    t = jnp.arange(T)
    row = (t // GRID_W).astype(F32)
    col = (t % GRID_W).astype(F32)
    half = HEAD_DIM // 2
    quarter = half // 2
    inv_freq = ROPE_THETA ** (-jnp.arange(quarter, dtype=F32) * 2.0 / half)

    def rotate(xa, pos):
        ang = pos[:, None] * inv_freq[None, :]
        cos = jnp.cos(ang)[None, :, None, :]
        sin = jnp.sin(ang)[None, :, None, :]
        x1, x2 = xa[..., :quarter], xa[..., quarter:]
        return jnp.concatenate([x1 * cos - x2 * sin, x2 * cos + x1 * sin], -1)

    xf = x.astype(F32)
    return jnp.concatenate([rotate(xf[..., :half], row), rotate(xf[..., half:], col)], -1).astype(x.dtype)

def short_conv(x, w):
    return lax.conv_general_dilated(x, w.astype(x.dtype)[:, None, :], window_strides=(1,),
                                    padding=[(CONV_W // 2, CONV_W // 2)],
                                    dimension_numbers=('NWC', 'WIO', 'NWC'),
                                    feature_group_count=x.shape[-1])

def to_chunks(x, c):
    B, T = x.shape[:2]
    x = x.reshape(B, T // c, c, *x.shape[2:])
    return jnp.moveaxis(x, (1, 3), (0, 2))

def from_chunks(o):
    o = jnp.moveaxis(o, (0, 2), (1, 3))
    return o.reshape(o.shape[0], -1, *o.shape[3:])

def masked_exp(mask, d):
    return jnp.where(mask, jnp.exp(jnp.where(mask, d, 0.0)), 0.0)

def gdn_scan(q, k, v, beta, log_alpha, s0):
    C = GDN_CHUNK
    tri_incl = jnp.tril(jnp.ones((C, C), bool))
    tri_strict = jnp.tril(jnp.ones((C, C), bool), -1)
    eye = jnp.eye(C, dtype=F32)

    def step(S, inp):
        qc, kc, vc, bc, ac = inp
        g = jnp.cumsum(ac, axis=-1)
        decay = masked_exp(tri_incl, g[..., :, None] - g[..., None, :])
        kb = kc * bc[..., None]
        L = jnp.where(tri_strict, jnp.einsum('bhik,bhjk->bhij', kb, kc) * decay, 0.0)
        Tm = lax.linalg.triangular_solve(eye + L, jnp.broadcast_to(eye, L.shape), left_side=True, lower=True)
        u = Tm @ (vc * bc[..., None])
        w = Tm @ (kb * jnp.exp(g)[..., None])
        v_new = u - w @ S
        attn = jnp.einsum('bhik,bhjk->bhij', qc, kc) * decay
        o = (qc * jnp.exp(g)[..., None]) @ S + attn @ v_new
        g_last = g[..., -1]
        S = S * jnp.exp(g_last)[..., None, None] + jnp.einsum(
            'bhck,bhcv->bhkv', kc * jnp.exp(g_last[..., None] - g)[..., None], v_new)
        return S, o

    xs = tuple(to_chunks(t.astype(F32), C) for t in (q, k, v, beta, log_alpha))
    S, o = lax.scan(step, s0.astype(F32), xs)
    return from_chunks(o), S

def hgrn_scan(q, k, v, log_f, s0):
    C = HGRN_CHUNK
    tri = jnp.tril(jnp.ones((C, C), bool))[:, :, None]

    def step(S, inp):
        qc, kc, vc, lf = inp
        b = jnp.cumsum(lf, axis=2)
        dec = masked_exp(tri, b[:, :, :, None, :] - b[:, :, None, :, :])
        A = jnp.einsum('bhik,bhjk,bhijk->bhij', qc, kc, dec)
        o = jnp.einsum('bhik,bhkv->bhiv', qc * jnp.exp(b), S) + A @ vc
        bl = b[:, :, -1]
        S = S * jnp.exp(bl)[..., None] + jnp.einsum('bhck,bhcv->bhkv', kc * jnp.exp(bl[:, :, None] - b), vc)
        return S, o

    xs = tuple(to_chunks(t.astype(F32), C) for t in (q, k, v, log_f))
    S, o = lax.scan(step, s0.astype(F32), xs)
    return from_chunks(o), S

def bidirectional(scan_fn, fwd_args, bwd_args, s0_fwd, s0_bwd):
    o_f, s_f = scan_fn(*fwd_args, s0_fwd)
    o_b, s_b = scan_fn(*[jnp.flip(t, axis=1) for t in bwd_args], s0_bwd)
    return o_f + jnp.flip(o_b, axis=1), jnp.stack([s_f, s_b], axis=1)

def softmax_with_sink(s, sink):
    snk = sink.astype(F32).reshape(A_KV_HEADS, A_HEADS // A_KV_HEADS)[:, :, None, None]
    m = jnp.maximum(jnp.max(s, -1, keepdims=True), snk)
    e = jnp.exp(s - m)
    return e / (jnp.sum(e, -1, keepdims=True) + jnp.exp(snk - m))

def attn_context(q, k, v, sink):
    B, L = q.shape[:2]
    R = A_HEADS // A_KV_HEADS
    nqb = L // ATTN_BLOCK
    qb = jnp.moveaxis(q.reshape(B, nqb, ATTN_BLOCK, A_KV_HEADS, R, HEAD_DIM), 1, 0)
    scale = HEAD_DIM ** -0.5

    def one_block(qblk):
        s = jnp.einsum('bqgrd,bkgd->bgrqk', qblk, k, preferred_element_type=F32) * scale
        p = softmax_with_sink(s, sink)
        return jnp.einsum('bgrqk,bkgd->bqgrd', p.astype(v.dtype), v)

    o = lax.map(one_block, qb)
    return jnp.moveaxis(o, 0, 1).reshape(B, L, D_A)

def attn_latent(q, k, v, ck, cv, sink):
    B, T = q.shape[:2]
    R = A_HEADS // A_KV_HEADS
    nb = T // ATTN_BLOCK
    pad = ((0, 0), (ATTN_BLOCK, ATTN_BLOCK), (0, 0), (0, 0))
    kp = jnp.pad(k, pad).reshape(B, nb + 2, ATTN_BLOCK, A_KV_HEADS, HEAD_DIM)
    vp = jnp.pad(v, pad).reshape(B, nb + 2, ATTN_BLOCK, A_KV_HEADS, HEAD_DIM)
    kband = jnp.concatenate([kp[:, :-2], kp[:, 1:-1], kp[:, 2:]], axis=2)
    vband = jnp.concatenate([vp[:, :-2], vp[:, 1:-1], vp[:, 2:]], axis=2)
    qb = q.reshape(B, nb, ATTN_BLOCK, A_KV_HEADS, R, HEAD_DIM)
    scale = HEAD_DIM ** -0.5
    s_loc = jnp.einsum('bnqgrd,bnkgd->bngrqk', qb, kband, preferred_element_type=F32) * scale
    s_ctx = jnp.einsum('bnqgrd,bkgd->bngrqk', qb, ck, preferred_element_type=F32) * scale
    blk = jnp.arange(nb)[:, None] * ATTN_BLOCK
    qpos = blk + jnp.arange(ATTN_BLOCK)[None, :]
    kpos = blk - ATTN_BLOCK + jnp.arange(3 * ATTN_BLOCK)[None, :]
    valid = ((kpos[:, None, :] >= 0) & (kpos[:, None, :] < T)
             & (jnp.abs(qpos[:, :, None] - kpos[:, None, :]) <= WINDOW))
    s_loc = jnp.where(valid[None, :, None, None], s_loc, MASK_VALUE)
    p = softmax_with_sink(jnp.concatenate([s_loc, s_ctx], -1), sink).astype(v.dtype)
    nk = 3 * ATTN_BLOCK
    o = (jnp.einsum('bngrqk,bnkgd->bnqgrd', p[..., :nk], vband)
         + jnp.einsum('bngrqk,bkgd->bnqgrd', p[..., nk:], cv))
    return o.reshape(B, T, D_A)

def prepare(h, w_in, conv_w, a_log, dt_bias, lb):
    B, T, _ = h.shape
    sizes = [D_A, D_KV, D_KV, 3 * D_B, D_B, 2 * B_HEADS, 2 * B_HEADS, D_C, D_C, D_C, D_C, D_C]
    bounds, acc = [], 0
    for s in sizes[:-1]:
        acc += s
        bounds.append(acc)
    qa, ka, va, qkv_b, g_b, beta_b, alpha_b, f_fw, f_bw, i_c, q_c, g_c = jnp.split(h @ w_in, bounds, axis=-1)

    def heads(t, n):
        return t.reshape(B, T, n, HEAD_DIM)

    attn = (heads(qa, A_HEADS), heads(ka, A_KV_HEADS), heads(va, A_KV_HEADS))
    qkv_b = jax.nn.silu(short_conv(qkv_b, conv_w))
    q_b, k_b, v_b = [heads(t, B_HEADS).astype(F32) for t in jnp.split(qkv_b, 3, axis=-1)]
    q_b = l2_normalize(q_b) * HEAD_DIM ** -0.5
    k_b = l2_normalize(k_b)
    beta = jax.nn.sigmoid(beta_b.astype(F32)).reshape(B, T, 2, B_HEADS)
    log_alpha = -jnp.exp(a_log.astype(F32)) * jax.nn.softplus(
        alpha_b.astype(F32).reshape(B, T, 2, B_HEADS) + dt_bias.astype(F32))
    gdn = (q_b, k_b, v_b, beta, log_alpha, heads(g_b, B_HEADS))
    z = jnp.stack([f_fw, f_bw], axis=2).astype(F32)
    f = lb + (1.0 - lb) * jax.nn.sigmoid(z)
    log_f = jnp.log(jnp.maximum(f, TINY)).reshape(B, T, 2, C_HEADS, HEAD_DIM)
    k_c = (1.0 - f).reshape(B, T, 2, C_HEADS, HEAD_DIM)
    hgrn = (heads(q_c, C_HEADS).astype(F32), k_c, heads(i_c, C_HEADS).astype(F32), log_f, heads(g_c, C_HEADS))
    return attn, gdn, hgrn

def recurrent_groups(gdn, hgrn, s_gdn, s_hgrn, gdn_norm_w, hgrn_norm_w, dtype):
    q_b, k_b, v_b, beta, log_alpha, g_b = gdn
    o_b, st_b = bidirectional(gdn_scan, (q_b, k_b, v_b, beta[:, :, 0], log_alpha[:, :, 0]),
                              (q_b, k_b, v_b, beta[:, :, 1], log_alpha[:, :, 1]), s_gdn[:, 0], s_gdn[:, 1])
    q_c, k_c, i_c, log_f, g_c = hgrn
    o_c, st_c = bidirectional(hgrn_scan, (q_c, k_c[:, :, 0], i_c, log_f[:, :, 0]),
                              (q_c, k_c[:, :, 1], i_c, log_f[:, :, 1]), s_hgrn[:, 0], s_hgrn[:, 1])
    out_b = gated_rms_readout(o_b, g_b, gdn_norm_w).astype(dtype)
    out_c = gated_rms_readout(o_c, g_c, hgrn_norm_w).astype(dtype)
    return out_b, out_c, st_b, st_c

def mixer_context(h, w_in, conv_w, a_log, dt_bias, lb, sink, gdn_norm_w, hgrn_norm_w, w_out):
    (qa, ka, va), gdn, hgrn = prepare(h, w_in, conv_w, a_log, dt_bias, lb)
    B = h.shape[0]
    o_a = attn_context(qa, ka, va, sink)
    z_b = jnp.zeros((B, 2, B_HEADS, HEAD_DIM, HEAD_DIM), F32)
    z_c = jnp.zeros((B, 2, C_HEADS, HEAD_DIM, HEAD_DIM), F32)
    o_b, o_c, st_b, st_c = recurrent_groups(gdn, hgrn, z_b, z_c, gdn_norm_w, hgrn_norm_w, h.dtype)
    y = jnp.concatenate([o_a, o_b, o_c], -1) @ w_out
    return y, ka, va, st_b, st_c

def mixer_latent(h, ck, cv, s_gdn, s_hgrn, w_in, conv_w, a_log, dt_bias, lb, sink, gdn_norm_w, hgrn_norm_w, w_out):
    (qa, ka, va), gdn, hgrn = prepare(h, w_in, conv_w, a_log, dt_bias, lb)
    o_a = attn_latent(rope_2d(qa), rope_2d(ka), va, ck, cv, sink)
    o_b, o_c, _, _ = recurrent_groups(gdn, hgrn, s_gdn, s_hgrn, gdn_norm_w, hgrn_norm_w, h.dtype)
    return jnp.concatenate([o_a, o_b, o_c], -1) @ w_out

def swiglu(h, w1, w3, w2):
    return (jax.nn.silu(h @ w1) * (h @ w3)) @ w2

def moe(h, w_r, b_r, w1, w3, w2):
    logits = (h @ w_r).astype(F32) + b_r.astype(F32)
    top_v, top_i = lax.top_k(logits, TOP_K)
    gates = jax.nn.softmax(top_v, axis=-1)
    combine = jnp.sum(jax.nn.one_hot(top_i, N_EXPERTS, dtype=F32) * gates[..., None], axis=-2).astype(h.dtype)
    y = jnp.zeros_like(h)
    for e in range(N_EXPERTS):
        y = y + combine[..., e:e + 1] * swiglu(h, w1[e], w3[e], w2[e])
    return y

def channel_mixer(l, h, ffn_w1, ffn_w3, ffn_w2, moe_router, moe_router_b, moe_w1, moe_w3, moe_w2):
    i = l // 2
    if l % 2 == 0:
        return swiglu(h, ffn_w1[i], ffn_w3[i], ffn_w2[i])
    return moe(h, moe_router[i], moe_router_b[i], moe_w1[i], moe_w3[i], moe_w2[i])

def hgrn_lower_bounds(lb_param):
    s = jax.nn.softmax(lb_param.astype(F32), axis=0)
    return jnp.cumsum(s, axis=0) - s[0:1]

def setup_inputs(seed: int = 0) -> dict:
    key = jax.random.key(seed)
    ks = jax.random.split(key, 32)

    def nrm(k, shape, s):
        return jax.random.normal(k, shape, F32) * s

    deep = (8.0 * DEPTH) ** -0.25
    n_dense = (DEPTH + 1) // 2
    n_moe = DEPTH // 2
    dt = jnp.exp(jax.random.uniform(ks[10], (DEPTH, 2, B_HEADS), F32, np.log(1e-3), np.log(1e-1)))
    return {
        'x_prompt': nrm(ks[0], (BATCH, SEQ, D_MODEL), 1.0),
        'x_sample': nrm(ks[1], (DEC_BATCH, DEC_SEQ, D_MODEL), 1.0),
        'cache_k': nrm(ks[2], (DEC_BATCH, DEPTH, PAST_LEN, A_KV_HEADS, HEAD_DIM), 1.0),
        'cache_v': nrm(ks[3], (DEC_BATCH, DEPTH, PAST_LEN, A_KV_HEADS, HEAD_DIM), 1.0),
        'state_gdn': nrm(ks[4], (DEC_BATCH, DEPTH, 2, B_HEADS, HEAD_DIM, HEAD_DIM), 0.1),
        'state_hgrn': nrm(ks[5], (DEC_BATCH, DEPTH, 2, C_HEADS, HEAD_DIM, HEAD_DIM), 0.5),
        'c': nrm(ks[6], (DEC_BATCH, D_MODEL), 1.0),
        'c_ctx': nrm(ks[7], (D_MODEL,), 1.0),
        'w_mod': nrm(ks[8], (DEPTH, D_MODEL, 6 * D_MODEL), 0.5 * D_MODEL ** -0.5),
        'b_mod': nrm(ks[9], (DEPTH, 6 * D_MODEL), 0.02),
        'w_in': nrm(ks[11], (DEPTH, D_MODEL, D_IN), D_MODEL ** -0.5),
        'conv_w': nrm(ks[12], (DEPTH, CONV_W, 3 * D_B), CONV_W ** -0.5),
        'attn_sink': nrm(ks[13], (DEPTH, A_HEADS), 0.5),
        'gdn_a_log': jnp.log(jax.random.uniform(ks[14], (DEPTH, 2, B_HEADS), F32, 1.0, 16.0)),
        'gdn_dt_bias': dt + jnp.log(-jnp.expm1(-dt)),
        'gdn_norm_w': 1.0 + nrm(ks[15], (DEPTH, HEAD_DIM), 0.02),
        'hgrn_lb': nrm(ks[16], (DEPTH, 2, D_C), 1.0),
        'hgrn_norm_w': 1.0 + nrm(ks[17], (DEPTH, HEAD_DIM), 0.02),
        'w_out': nrm(ks[18], (DEPTH, D_MIX, D_MODEL), deep * D_MIX ** -0.5),
        'ln_g': 1.0 + nrm(ks[19], (DEPTH, 2, D_MODEL), 0.02),
        'ln_b': nrm(ks[20], (DEPTH, 2, D_MODEL), 0.02),
        'ffn_w1': nrm(ks[21], (n_dense, D_MODEL, D_FF), D_MODEL ** -0.5),
        'ffn_w3': nrm(ks[22], (n_dense, D_MODEL, D_FF), D_MODEL ** -0.5),
        'ffn_w2': nrm(ks[23], (n_dense, D_FF, D_MODEL), deep * D_FF ** -0.5),
        'moe_router': nrm(ks[24], (n_moe, D_MODEL, N_EXPERTS), D_MODEL ** -0.5),
        'moe_router_b': nrm(ks[25], (n_moe, N_EXPERTS), 0.01),
        'moe_w1': nrm(ks[26], (n_moe, N_EXPERTS, D_MODEL, EXPERT_FF), D_MODEL ** -0.5),
        'moe_w3': nrm(ks[27], (n_moe, N_EXPERTS, D_MODEL, EXPERT_FF), D_MODEL ** -0.5),
        'moe_w2': nrm(ks[28], (n_moe, N_EXPERTS, EXPERT_FF, D_MODEL), deep * EXPERT_FF ** -0.5),
    }

def reference(x_prompt, x_sample, cache_k, cache_v, state_gdn, state_hgrn, c, c_ctx,
              w_mod, b_mod, w_in, conv_w, attn_sink, gdn_a_log, gdn_dt_bias, gdn_norm_w,
              hgrn_lb, hgrn_norm_w, w_out, ln_g, ln_b, ffn_w1, ffn_w3, ffn_w2,
              moe_router, moe_router_b, moe_w1, moe_w3, moe_w2):
    alpha = (2.0 * DEPTH) ** 0.25
    lower_bounds = hgrn_lower_bounds(hgrn_lb)
    xp, xs = x_prompt, x_sample
    new_k, new_v, new_sg, new_sh = [], [], [], []
    for l in range(DEPTH):
        mix_w = (w_in[l], conv_w[l], gdn_a_log[l], gdn_dt_bias[l], lower_bounds[l], attn_sink[l],
                 gdn_norm_w[l], hgrn_norm_w[l], w_out[l])
        ffn_w = (ffn_w1, ffn_w3, ffn_w2, moe_router, moe_router_b, moe_w1, moe_w3, moe_w2)
        sh1, sc1, g1, sh2, sc2, g2 = modulation(c_ctx, w_mod[l], b_mod[l])
        mix, k_l, v_l, s_b, s_c = mixer_context(xp * (1 + sc1) + sh1, *mix_w)
        xp = layer_norm(alpha * xp + g1 * mix, ln_g[l, 0], ln_b[l, 0])
        xp = layer_norm(alpha * xp + g2 * channel_mixer(l, xp * (1 + sc2) + sh2, *ffn_w), ln_g[l, 1], ln_b[l, 1])
        new_k.append(k_l)
        new_v.append(v_l)
        new_sg.append(s_b.astype(xp.dtype))
        new_sh.append(s_c.astype(xp.dtype))
        sh1, sc1, g1, sh2, sc2, g2 = modulation(c, w_mod[l], b_mod[l])
        mix = mixer_latent(xs * (1 + sc1) + sh1, cache_k[:, l], cache_v[:, l], state_gdn[:, l], state_hgrn[:, l], *mix_w)
        xs = layer_norm(alpha * xs + g1 * mix, ln_g[l, 0], ln_b[l, 0])
        xs = layer_norm(alpha * xs + g2 * channel_mixer(l, xs * (1 + sc2) + sh2, *ffn_w), ln_g[l, 1], ln_b[l, 1])
    new_cache_k = jnp.stack(new_k, axis=1)
    new_cache_v = jnp.stack(new_v, axis=1)
    new_state_gdn = jnp.stack(new_sg, axis=1)
    new_state_hgrn = jnp.stack(new_sh, axis=1)
    return (xp, xs, new_cache_k, new_cache_v, new_state_gdn, new_state_hgrn)


_drawn_inputs = setup_inputs


def setup_inputs(seed=0):
    import zlib

    import numpy as np

    out = dict(_drawn_inputs(seed))
    spreads = {}
    factors = {'cache_k': 8.0,
     'cache_v': 8.0,
     'state_gdn': 8.0,
     'state_hgrn': 8.0,
     'attn_sink': 54.599,
     'gdn_norm_w': 55.814,
     'hgrn_norm_w': 56.893,
     'moe_router_b': 34.908}
    for name, (base, spread) in spreads.items():
        noise = np.random.default_rng([zlib.crc32(name.encode()), seed]).standard_normal(out[name].shape)
        drawn = base * np.exp(spread * noise) if base else spread * noise
        out[name] = __import__('jax').numpy.asarray(drawn.astype(out[name].dtype))
    for name, factor in factors.items():
        out[name] = (out[name] * factor).astype(out[name].dtype)
    return out
```

```python
from contextlib import ExitStack

import numpy as np

import concourse.bass as bass
from concourse import mybir

ALU = mybir.AluOpType
ACT = mybir.ActivationFunctionType
F32 = mybir.dt.float32
AX_X = mybir.AxisListType.X

P = 128
D = 1024
KT = D // P
LAT = 512
CTX = 128
NT = LAT + CTX
TT = NT // P
DEPTH = 2
HD = 64
D_IN = 3088
D_FF = 2816
NE = 8
EFF = 1024
CONV = 5
PADW = NT + 6
CVW = NT + 2
SLAB = 256
LEV = 7
SLOTS = 4
ALPHA = (2.0 * DEPTH) ** 0.25
ATT_SCALE = HD ** -0.5
OFF_BA, OFF_F, OFF_I, OFF_QC, OFF_GC, OFF_GB, OFF_B, OFF_KV = 1792, 1808, 2320, 2576, 2832, 1536, 768, 512

_WIDTH = [("ident", P), ("mean", 1), ("blk", P), ("rot", P), ("cos", LAT), ("sin", LAT), ("hg", 2 * 8 * P),
          ("mk", 2 * 8 * P), ("rev", 2 * P), ("am", 5 * P), ("tie", 64)]
CONST_AT = {}
_at = 0
for _n, _w in _WIDTH:
    CONST_AT[_n] = (_at, _w)
    _at += _w
NCONST = _at


def constant_table():
    t = np.zeros((P, NCONST), np.float32)

    def put(name, a):
        o, w = CONST_AT[name]
        t[:, o:o + w] = np.asarray(a, np.float32).reshape(P, w)

    put("ident", np.eye(P))
    put("mean", np.full((P, 1), 1.0 / D))
    i = np.arange(P)
    put("blk", (i[:, None] // HD) == (i[None, :] // HD))
    rot = np.zeros((P, P))
    for m in range(P):
        if m % 32 < 16:
            rot[m + 16, m] = -1.0
        else:
            rot[m - 16, m] = 1.0
    put("rot", rot)
    inv = np.float32(10000.0) ** (-np.arange(16, dtype=np.float32) * np.float32(2.0) / np.float32(32))
    tok = np.arange(LAT)
    pos = np.where(((i % HD) // 32 == 0)[:, None], (tok // 64)[None, :], (tok % 64)[None, :]).astype(np.float32)
    ang = (pos * inv[i % 16][:, None]).astype(np.float32)
    put("cos", np.cos(ang))
    put("sin", np.sin(ang))
    a, b = i[:, None], i[None, :]
    hg = np.zeros((P, 8, P))
    mk = np.zeros((P, 8, P))
    for lev in range(LEV):
        s = 1 << lev
        mid = (b // (2 * s)) * 2 * s + s - 1
        right = (b % (2 * s)) >= s
        hg[:, lev] = np.where(right, (a > mid) & (a <= b), (a > b) & (a <= mid))
        mk[:, lev] = (a // (2 * s) == b // (2 * s)) & ((a % (2 * s)) < s) & right
    hg[:, 7] = a <= b
    mk[:, 7] = a == b
    put("hg", np.stack([hg, hg[::-1, :, ::-1]], 1))
    put("mk", np.stack([mk, mk[::-1, :, ::-1]], 1))
    put("rev", np.stack([a > b, a < b], 1))
    zero = np.zeros((P, P))
    before = np.where(b >= a, 0.0, -1e30)
    after = np.where(b <= a, 0.0, -1e30)
    put("am", np.stack([zero, before, zero, after, zero], 1))
    e = np.arange(8)
    put("tie", np.broadcast_to((e[None, :] < e[:, None]).reshape(1, 64), (P, 64)))
    return t


def chunk(d, n):
    return 4 if n == 4 else (n if d == 0 else 3 - n)


def cv_col(c):
    return c * P + (2 if c == 4 else 0)


def psum_plan():
    names = [f"xt{t}" for t in range(TT)] + ["par"]
    loops = {}
    for l in range(DEPTH):
        j = [f"mod"] + [f"q{t}" for t in range(4)] + ["ka", "va"] + [f"b{t}" for t in range(6)]
        j += ["gb0", "gb1", "ba", "f0a", "f0b", "f1a", "f1b", "ia", "ib", "qc0", "qc1", "gc0", "gc1", "kout", "ckt"]
        j += [f"rot{t}" for t in range(5)]
        units = [f"{n}_{t}" for n in range(5) for t in range(4)]
        for x in range(len(units) + 1):
            if x < len(units):
                j.append("S" + units[x])
            if x >= 1:
                j += ["T" + units[x - 1], "O" + units[x - 1]]
        j += [f"l2{t}" for t in range(4)] + [f"kv{t}" for t in range(TT)] + ["gate"]
        for n in range(5):
            j += [f"grow{n}", f"brow{n}", f"G{n}", f"KQ{n}"]
            for v in range(LEV):
                j += [f"W{n}_{v}"] + ([f"T{n}__{v}"] if 0 < v < LEV - 1 else []) + ([f"TT{n}_{v}"] if v else [])
            j += [f"uw{n}", f"vn{n}", f"gs{n}"]
        for n in range(5):
            j += [f"hk{n}"]
            for x in range(5):
                if x < 4:
                    j.append(f"E{n}_{x}")
                if x >= 1:
                    j += [f"P{n}_{x - 1}_0", f"P{n}_{x - 1}_1"]
            j += [f"hs{n}"]
        j += [f"rs{t}" for t in range(4)] + [f"wo{m}" for m in range(KT)] + ["mean1", "var1"]
        if l % 2:
            j += ["router"] + [f"cb{e}" for e in range(NE)]
        names += [f"{l}.{x}" for x in j]
        while len(names) % SLOTS:
            names.append(None)
        loops[l] = len(names)
        names += [f"{l}.ffn"] * (12 * (NE * EFF // SLAB if l % 2 else D_FF // SLAB))
        names += [f"{l}.mean2", f"{l}.var2"]
    names += [f"yt{t}" for t in range(TT)]
    plan, turns, base = {}, [0] * SLOTS, {}
    for n, name in enumerate(names):
        for l, at in loops.items():
            if n == at:
                base[l] = list(turns)
        if name is None:
            continue
        plan[name] = (n % SLOTS, turns[n % SLOTS])
        turns[n % SLOTS] += 1
    return plan, base


def weight_plan():
    names, loops = [], {}
    for l in range(DEPTH):
        j = [f"mod{i}" for i in range(24)] + ["qa0", "qa1", "kv", "b0", "b1", "b2", "gb", "ba", "f0", "f1", "i", "qc", "gc"]
        j += [f"wo{i}" for i in range(4)]
        names += [f"{l}.{x}" for x in j]
        while len(names) % 3:
            names.append(None)
        loops[l] = len(names)
        names += [f"{l}.ffn"] * (3 * (NE * EFF // SLAB if l % 2 else D_FF // SLAB))
    plan, turns, base = {}, [0] * 3, {}
    for n, name in enumerate(names):
        for l, at in loops.items():
            if n == at:
                base[l] = list(turns)
        if name is None:
            continue
        plan[name] = (n % 3, turns[n % 3])
        turns[n % 3] += 1
    return plan, base, [n for n in names if n]


def release(l, what):
    if what.startswith("wo"):
        return f"{l}.wo{2 * int(what[2]) + 1}"
    return f"{l}." + {"mod23": "mod", "qa0": "q1", "qa1": "q3", "kv": "va", "b0": "b1", "b1": "b3", "b2": "b5",
                      "gb": "gb1", "ba": "ba", "f0": "f0b", "f1": "f1b", "i": "ib", "qc": "qc1", "gc": "gc1"}[what]


def backbone_kernel(nc, x_prompt, x_sample, cache_k, cache_v, state_gdn, state_hgrn, c, c_ctx, w_mod, b_mod, w_in,
                    conv_w, attn_sink, gdn_a_log, gdn_dt_bias, gdn_norm_w, hgrn_lb, hgrn_norm_w, w_out, ln_g, ln_b,
                    ffn_w1, ffn_w3, ffn_w2, moe_router, moe_router_b, moe_w1, moe_w3, moe_w2, table,
                    y_prompt, y_sample, new_k, new_v, new_sg, new_sh):
    PS, PS_BASE = psum_plan()
    WP, WP_BASE, WNAMES = weight_plan()
    SLABS = [D_FF // SLAB, NE * EFF // SLAB]
    ES = EFF // SLAB
    ctx = ExitStack()
    with ctx:
        def sb(name, shape):
            return ctx.enter_context(nc.sbuf_tensor(name, shape, F32))

        def sem(name):
            return ctx.enter_context(nc.semaphore(name))

        const = sb("const", [P, NCONST])
        xT = sb("xT", [P, KT, NT])
        hT = sb("hT", [P, KT, NT])
        arena = sb("arena", [P, KT * NT + 5 * NT])
        extra = sb("extra", [P, 2560])
        wbuf = sb("wbuf", [P, 3, 2048])
        PADN, CVN = 6 * PADW, 6 * CVW
        mix = sb("mix", [P, PADN + CVN + 6 * NT + TT * 768])
        va = sb("va", [P, TT, P])
        cachek = sb("cachek", [P, P])
        cachekT = sb("cachekT", [P, P])
        cachev = sb("cachev", [P, P])
        koutb = sb("koutb", [P, P])
        ba = sb("ba", [P, TT, 16])
        gates = sb("gates", [P, 8, 2, 20])
        SG = sb("SG", [P, 4, P])
        SH = sb("SH", [P, 4, P])
        modT = sb("modT", [P, 48, 2])
        par = sb("par", [P, 3 * P])
        sink = sb("sink", [P, DEPTH * 8])
        alog = sb("alog", [P, DEPTH * 8])
        dtb = sb("dtb", [P, DEPTH * 8])
        lbt = sb("lbt", [P, 512])
        siluc = sb("siluc", [P, 16])
        small = sb("small", [P, 2, 16])
        eps = sb("eps", [P, 2])
        wr = sb("wr", [P, KT, NE])
        brr = sb("brr", [P, NE])
        ebl = sb("ebl", [P, 4])
        ps = ctx.enter_context(nc.psum_tensor("ps", [P, SLOTS, 1024], F32))

        def mem(t, at, *shape):
            v = t[:, at:at + int(np.prod(shape))]
            if len(shape) == 2:
                return v.rearrange("p (a b) -> p a b", a=shape[0])
            if len(shape) == 3:
                return v.rearrange("p (a b c) -> p a b c", a=shape[0], b=shape[1])
            return v

        def cst(name, *shape):
            o, w = CONST_AT[name]
            return mem(const, o, *(shape + (w // int(np.prod(shape)),)))

        ident, blk, rot, cosT, sinT, am, tie = (cst(n) for n in ("ident", "blk", "rot", "cos", "sin", "am", "tie"))
        mean = cst("mean").broadcast_to([P, P])
        hg, mk, rev = cst("hg", 2, 8), cst("mk", 2, 8), cst("rev", 2)
        inc = hg[:, :, 7]

        pad = mem(mix, 0, 6, PADW)
        ktok = mem(mix, 0, TT, 256)
        vtok = mem(mix, TT * 256, TT, 256)
        kd = mem(mix, 2 * TT * 256, 8, HD)
        qg = mem(mix, 2 * TT * 256 + 512, 4, P)
        cv = mem(mix, PADN, 6, CVW)
        u_b = mem(mix, PADN + 4 * CVW, 8, HD)
        wT_b = mem(mix, PADN + 4 * CVW + 512, 4, P)
        gbc = mem(mix, PADN + CVN, 4, NT)
        qc = mem(mix, PADN + CVN + 4 * NT, 2, NT)
        lf = mem(mix, PADN + CVN + 6 * NT, TT, 512)
        lfd = mem(mix, PADN + CVN + 6 * NT, TT * 512)
        iv = mem(mix, PADN + CVN + 6 * NT + TT * 512, TT, 256)
        combB = mem(mix, 0, NE, NT)
        gbuf = mem(mix, NE * NT, 2, NT)
        abuf = mem(mix, NE * NT + 2 * NT, 2, NT)
        rstd = mem(mix, NE * NT + 4 * NT, NT)
        rt = NE * NT + 5 * NT
        lg, top, comb, first = (mem(mix, rt + 40 * i, TT, NE) for i in range(4))
        ggt, geq = (mem(mix, rt + 160 + 320 * i, TT, NE, NE) for i in range(2))
        tq = mem(mix, rt + 800, 3, TT)

        yacc = mem(arena, 0, KT, NT)
        xin = mem(arena, 0, TT, D)
        qk = mem(arena, KT * NT, 5, NT)
        a_s = [mem(arena, 1024 * i, 2, 512) for i in range(2)]
        a_pT = [mem(arena, 2048 + 1024 * i, 2, 512) for i in range(2)]
        lf2 = mem(arena, 0, TT * 512)
        sqb = mem(arena, 0, 4, CVW)
        rsb = [mem(arena, 4 * CVW + CVW * i, CVW) for i in range(2)]
        osq = mem(arena, 0, 4, NT)
        orb = [mem(arena, (4 + i) * NT, NT) for i in range(2)]
        EG, DM, LT, T_, Tt, Wb, AT = [mem(arena, 1024 * i, 8, P) for i in range(7)]
        vb = mem(arena, 7168, 8, HD)
        kbg = mem(arena, 7680, 8, HD)
        CS = [mem(extra, 1024 * i, 8, P) for i in range(2)]
        vnew = mem(extra, 2048, 8, HD)
        Eb = [mem(arena, 1024 * i, 8, P) for i in range(2)]
        QE = [mem(arena, 2048 + 896 * i, 7, P) for i in range(2)]
        KE = [mem(arena, 3840 + 896 * i, 7, P) for i in range(2)]
        PM = mem(arena, 5632, 8, P)
        AH = mem(arena, 6656, 8, P)
        QB = mem(arena, 7680, 4, P)
        KK = mem(extra, 0, 2, 256)
        KTt = mem(extra, 512, 4, P)
        KD = mem(extra, 1024, 2, 256)
        RV = mem(extra, 1536, 2, 256)
        lbrow = mem(extra, 0, 2, 512)
        rows = mem(extra, 1024, 3, P)
        LA, BETA, ZA, SP, BG, EGL, GC, EGC = (gates[:, i] for i in range(8))

        w_full = [sem(f"w_full{i}") for i in range(3)]
        ps_full = [sem(f"ps_full{i}") for i in range(SLOTS)]
        ps_free = [sem(f"ps_free{i}") for i in range(SLOTS)]
        sg = {n: sem(n) for n in (
            "act_chain dve_chain pool_chain "
            "tab_in x_in cache_in state_in out_done yt_out rows_clear s_clear mod_used "
            "siluc_ready lb_in lb_exp h_ready pad_zero conv_done conv_silu rope_ready sm_in sm_exp prob_ready "
            "f_in f_ln lf_ready l2_sq l2_r l2_ready ab_in ab_exp la_ready g_ready "
            "eg_ready dm_in dm_exp vk_ready cs_ready t_ready "
            "kk_exp kk_ready kd_ready qe_ready ke_ready ah_ready o_zero o_sq r_ready o_ready "
            "z_ready sq_ready rstd_ready xn_ready v_in v_exp comb_ready g_comb").split()}
        OUTS = 16 * 6

        block = ctx.enter_context(nc.Block())

        class Lane:

            def __init__(self, eng, chain):
                self.eng, self.chain, self.made, self.took = eng, chain, {}, {}

            def do(self, ins, to=None):
                s = to or self.chain
                self.made[s] = self.made.get(s, 0) + 1
                ins.then_inc(sg[s], 1)
                self.eng.wait_ge(sg[s], self.made[s])

            def need(self, s, n=1):
                self.took[s] = self.took.get(s, 0) + n
                self.eng.wait_ge(sg[s], self.took[s])

            def full(self, job):
                slot, turn = PS[job]
                self.eng.wait_ge(ps_full[slot], turn + 1)
                return ps[:, slot]

            def free(self, ins, job):
                slot, turn = PS[job]
                ins.then_inc(ps_free[slot], 1)
                self.eng.wait_ge(ps_free[slot], turn + 1)

            def done(self, job):
                slot, turn = PS[job]
                self.eng.wait_ge(ps_free[slot], turn + 1)

        def wpiece(slot, n=256):
            return wbuf[:, slot, 0:8 * n].rearrange("p (k n) -> p k n", k=KT)

        def heads_of(state, f):
            return state.rearrange("d (r f) k v -> f k (d r) v", f=2)[f]

        def diag(S, f):
            return S[f * HD:(f + 1) * HD, :, f * HD:(f + 1) * HD]

        def per_half(v, f):
            return v[:, 4 * f:4 * f + 4].rearrange("p (d r) i -> p d r i", d=2)

        def per_dir(v, d):
            return v.rearrange("p (f e r) i -> p f e r i", f=2, e=2)[:, :, d]

        def gate_of(v, d, c):
            return v[:, d, 4 * c:4 * c + 4].rearrange("p (r f) -> p f r", r=2)

        def last_row(d):
            return P - 1 if d == 0 else 0

        xo = [(x_sample, t * P) for t in range(4)] + [(x_prompt, 0)]
        yo = [(y_sample, t * P) for t in range(4)] + [(y_prompt, 0)]
        groups = ((0, 0, LAT), (1, LAT, NT))

        def window(n):
            if n == 4:
                return None, 0, P, LAT, None
            if n == 0:
                return 2 * P, 0, 3 * P, 0, 2 * P
            return 0, P, (4 if n < 3 else 3) * P, (n - 1) * P, 0

        units = [(n, t) for n in range(5) for t in range(4)]

        @block.sync
        def _(sp):
            sp.dma_start(const[:, :], table).then_inc(sg["tab_in"], 16)
            for t in range(TT):
                src, r = xo[t]
                sp.dma_start(xin[:, t, :], src[0, r:r + P, :]).then_inc(sg["x_in"], 16)
            last = [None] * 3

            def freed(slot):
                if last[slot] is None:
                    return
                l, what = last[slot]
                if what == "ffn":
                    bank, k = ((1, 1), (3, 1), (3, 3))[slot]
                    sp.wait_ge(ps_full[bank], PS_BASE[l][bank] + 3 * (SLABS[l] - 1) + k)
                elif what.startswith("mod") and what != "mod23":
                    sp.wait_ge(sg["mod_used"], 23 * l + int(what[3:]) + 1)
                else:
                    bank, turn = PS[release(l, what)]
                    sp.wait_ge(ps_full[bank], turn + 1)

            def fetch(name):
                slot, turn = WP[name]
                l, what = int(name[0]), name[2:]
                freed(slot)
                last[slot] = (l, what)
                dst = wpiece(slot)

                def cols(w, off, n):
                    return w[l].rearrange("(k p) n -> p k n", p=P)[:, :, off:off + n]

                if what.startswith("mod"):
                    parts = [(dst, cols(w_mod, int(what[3:]) * 256, 256))]
                elif what.startswith("qa"):
                    v = dst.rearrange("p k (t g j) -> p k t g j", t=2, g=2)
                    parts = [(v[:, :, t, g, :], cols(w_in, (g * 4 + int(what[2]) * 2 + t) * HD, HD))
                             for t in range(2) for g in range(2)]
                elif what.startswith("wo"):
                    src = w_out[l][:, int(what[2]) * 256:int(what[2]) * 256 + 256]
                    parts = [(dst[g * HD:(g + 1) * HD, 0:4, :],
                              src[g * 256:(g + 1) * 256, :].rearrange("(t j) n -> j t n", j=HD)) for g in range(2)]
                    parts += [(dst[:, k:k + 2, :], src[k * P:(k + 2) * P, :].rearrange("(k p) n -> p k n", p=P))
                              for k in (4, 6)]
                elif what == "ba":
                    parts = [(wpiece(slot, 16), cols(w_in, OFF_BA, 16))]
                else:
                    off = {"kv": OFF_KV, "b0": OFF_B, "b1": OFF_B + 256, "b2": OFF_B + 512, "gb": OFF_GB, "f0": OFF_F,
                           "f1": OFF_F + 256, "i": OFF_I, "qc": OFF_QC, "gc": OFF_GC}[what]
                    parts = [(dst, cols(w_in, off, 256))]
                for o, i in parts:
                    sp.dma_start(o, i).then_inc(w_full[slot], 64 // len(parts))

            def slab(l, w1, w3, w2, i):
                for slot, src, dst in ((0, w1, wpiece(0)), (1, w3, wpiece(1)),
                                       (2, w2, wbuf[:, 2, :].rearrange("p (t n) -> p t n", t=2))):
                    bank, k = ((1, 1), (3, 1), (3, 3))[slot]
                    sp.wait_ge(ps_full[bank], i * 3 + (PS_BASE[l][bank] - 3 + k))
                    sp.dma_start(dst, src).then_inc(w_full[slot], 64)

            for l in range(DEPTH):
                for name in WNAMES:
                    if name[0] == str(l) and not name.endswith("ffn"):
                        fetch(name)
                    if name == f"{l}.kv":
                        if l:
                            sp.wait_ge(sg["out_done"], OUTS * l)
                        else:
                            sp.wait_ge(sg["s_clear"], 1)
                        for S, st in ((SG, state_gdn), (SH, state_hgrn)):
                            for f in range(2):
                                sp.dma_start(diag(S, f), heads_of(st[0, l], f)).then_inc(sg["state_in"], 16)
                for slot in range(3):
                    freed(slot)
                    last[slot] = (l, "ffn")
                if l % 2 == 0:
                    w1 = ffn_w1[0].rearrange("(k p) (s n) -> p s k n", p=P, n=SLAB)
                    w3 = ffn_w3[0].rearrange("(k p) (s n) -> p s k n", p=P, n=SLAB)
                    w2 = ffn_w2[0].rearrange("(s t p) n -> p s t n", p=P, t=2)
                    with sp.Fori(0, SLABS[0]) as s:
                        slab(l, w1[:, s], w3[:, s], w2[:, s], s)
                else:
                    w1 = moe_w1[0].rearrange("e (k p) (s n) -> p e s k n", p=P, n=SLAB)
                    w3 = moe_w3[0].rearrange("e (k p) (s n) -> p e s k n", p=P, n=SLAB)
                    w2 = moe_w2[0].rearrange("e (s t p) n -> p e s t n", p=P, t=2)
                    with sp.Fori(0, NE) as e:
                        with sp.Fori(0, ES) as s:
                            slab(l, w1[:, e, s], w3[:, e, s], w2[:, e, s], e * ES + s)
            L = Lane(sp, None)
            for t in range(TT):
                L.done(f"yt{t}")
                dst, r = yo[t]
                sp.dma_start(dst[0, r:r + P, :], xin[:, t, :]).then_inc(sg["yt_out"], 16)
            sp.wait_ge(sg["yt_out"], 16 * TT)
            sp.wait_ge(sg["out_done"], OUTS * DEPTH)

        @block.gpsimd
        def _(pool):
            L = Lane(pool, "pool_chain")
            g = nc.gpsimd
            L.do(g.memset(rows[:, :, :], 0.0), "rows_clear")
            L.do(g.memset(SG[:, :, :], 0.0))
            L.do(g.memset(SH[:, :, :], 0.0), "s_clear")
            for l in range(DEPTH):
                L.need("h_ready")
                if l:
                    pool.wait_ge(sg["out_done"], OUTS * l)
                pool.dma_start(cachek[:, :], cache_k[0, l].rearrange("t g d -> t (g d)")).then_inc(sg["cache_in"], 16)
                pool.dma_start(cachev[:, :], cache_v[0, l].rearrange("t g d -> t (g d)")).then_inc(sg["cache_in"], 16)
                L.do(g.memset(mem(mix, 0, PADN), 0.0), "pad_zero")
                L.done(f"{l}.kout")
                pool.dma_start(new_k[0, l].rearrange("t g d -> t (g d)"), koutb[:, :]).then_inc(sg["out_done"], 16)
                pool.dma_start(new_v[0, l].rearrange("t g d -> t (g d)"), va[:, 4, :]).then_inc(sg["out_done"], 16)
                L.full(f"{l}.gc1")
                L.do(g.memset(hT[:, 4:8, :], 0.0), "o_zero")
                L.need("conv_silu")
                L.need("lf_ready")
                L.do(g.tensor_tensor(sqb, cv[:, 0:4, :], cv[:, 0:4, :], ALU.mult), "l2_sq")
                L.need("g_ready")
                L.done(f"{l}.kv4")
                for n in range(5):
                    if n:
                        L.done(f"{l}.gs{n - 1}")
                    for d in range(2):
                        cc = chunk(d, n)
                        for dst, src, sc in ((vb, vtok, BETA), (kbg, ktok, BG), (kd, ktok, EGL)):
                            L.do(g.tensor_tensor(per_dir(dst, d), src[:, cc].rearrange("p (r f j) -> p f r j", r=2, f=2),
                                                 gate_of(sc, d, cc).unsqueeze(3).broadcast_to([P, 2, 2, HD]), ALU.mult))
                    L.need("eg_ready")
                    for f in range(2):
                        r0, r1 = f * HD, (f + 1) * HD
                        for d in range(2):
                            cc = cv_col(chunk(d, n))
                            L.do(g.tensor_tensor(qg[r0:r1, 2 * d:2 * d + 2, :], cv[r0:r1, 0:2, cc:cc + P],
                                                 EG[r0:r1, f * 4 + 2 * d:f * 4 + 2 * d + 2, :], ALU.mult),
                                 "vk_ready" if f and d else None)
                    L.done(f"{l}.G{n}")
                    for v in range(LEV):
                        if v == 2:
                            L.need("t_ready")
                        if v > 2:
                            L.done(f"{l}.TT{n}_{v - 2}")
                        for f in range(2):
                            L.do(g.tensor_tensor(per_half(CS[v % 2], f), per_half(LT, f),
                                                 mk[:, :, v].unsqueeze(2).broadcast_to([P, 2, 2, P]), ALU.mult),
                                 "cs_ready" if f else None)
                L.done(f"{l}.gs4")
                for n in range(5):
                    L.done(f"{l}.hk{n}")
                    L.do(g.tensor_tensor(KD, KK, RV, ALU.mult), "kd_ready")
                    for x in range(4):
                        L.done(f"{l}.E{n}_{x}")
                        if x >= 2:
                            L.done(f"{l}.P{n}_{x - 2}_1")
                        L.do(g.tensor_tensor(KE[x % 2], Eb[x % 2][:, 0:7, :],
                                             KTt[:, x].unsqueeze(1).broadcast_to([P, 7, P]), ALU.mult), "ke_ready")
                    L.done(f"{l}.hs{n}")
                for S, dst in ((SG, new_sg), (SH, new_sh)):
                    for f in range(2):
                        pool.dma_start(heads_of(dst[0, l], f), diag(S, f)).then_inc(sg["out_done"], 16)
                L.do(g.tensor_tensor(osq, hT[:, 4:8, :], hT[:, 4:8, :], ALU.mult), "o_sq")
                if l % 2:
                    base = PS_BASE[l]
                    for e in range(NE):
                        with pool.Fori(0, ES) as s:
                            for t in range(2):
                                pool.wait_ge(ps_free[t], s * 3 + (base[t] + 1 + 3 * ES * e))
                                g.tensor_tensor(gbuf[:, t], gbuf[:, t], combB[:, e], ALU.mult).then_inc(sg["g_comb"], 1)

        @block.scalar
        def _(act):
            L = Lane(act, "act_chain")
            a = nc.scalar

            def copy(dst, src, job=None):
                ins = a.activation(dst, src, ACT.Copy)
                L.free(ins, job) if job else L.do(ins)

            L.need("rows_clear")
            par_in = [(rows[0:96, 0, :], b_mod.rearrange("l (t p) -> (l t) p", p=P)),
                      (rows[96:104, 0, :], c[0].rearrange("(k p) -> k p", p=P)),
                      (rows[104:112, 0, :], c_ctx.rearrange("(k p) -> k p", p=P)),
                      (rows[0:32, 1, :], ln_g.rearrange("l i (k p) -> (l i k) p", p=P)),
                      (rows[32:64, 1, :], ln_b.rearrange("l i (k p) -> (l i k) p", p=P)),
                      (rows[64:124, 1, :], conv_w.rearrange("l w (t p) -> (l w t) p", p=P))]
            par_in += [(rows[2 * i:2 * i + 2, 2, f * HD:(f + 1) * HD], w)
                       for i, w in enumerate((gdn_norm_w, hgrn_norm_w)) for f in range(2)]
            par_in += [(sink[:, :], attn_sink.rearrange("l h -> (l h)").partition_broadcast(P)),
                       (alog[:, :], gdn_a_log.rearrange("l d h -> (l d h)").partition_broadcast(P)),
                       (dtb[:, :], gdn_dt_bias.rearrange("l d h -> (l d h)").partition_broadcast(P)),
                       (lbrow.rearrange("p l n -> p (l n)"), hgrn_lb.rearrange("l d n -> (l d n)").partition_broadcast(P)),
                       (brr[:, :], moe_router_b[0].partition_broadcast(P)),
                       (wr[:, :, :], moe_router[0].rearrange("(k p) e -> p k e", p=P))]
            assert len(par_in) == PAR_DMAS
            for o, i in par_in:
                act.dma_start(o, i).then_inc(sg["tab_in"], 16)
            for t in range(TT):
                s = L.full(f"xt{t}")
                copy(xT[:, :, t * P:(t + 1) * P], s.rearrange("p (k i) -> p k i", k=KT), f"xt{t}")
            copy(par[:, :], L.full("par")[:, 0:3 * P], "par")
            L.do(a.activation(siluc[:, :], par[:, 96:112], ACT.Silu), "siluc_ready")
            L.need("lb_in")
            L.do(a.activation(lbrow, lbrow, ACT.Exp))
            L.do(a.activation(alog[:, :], alog[:, :], ACT.Exp), "lb_exp")

            for l in range(DEPTH):
                J = lambda name: f"{l}.{name}"
                L.need("h_ready")
                if l:
                    act.wait_ge(sg["out_done"], OUTS * l)
                for t in range(4):
                    copy(qk[:, t, :], L.full(J(f"q{t}"))[:, 0:NT], J(f"q{t}"))
                copy(qk[:, 4, :], L.full(J("ka"))[:, 0:NT], J("ka"))
                copy(va[:, :, :], L.full(J("va"))[:, 0:NT].rearrange("p (t n) -> p t n", t=TT), J("va"))
                for t in range(2):
                    L.free(a.activation(gbc[:, t, :], L.full(J(f"gb{t}"))[:, 0:NT], ACT.Silu), J(f"gb{t}"))
                for h in range(2):
                    for part, t0, t1 in (("a", 0, 4), ("b", 4, 5)):
                        j = J(f"f{h}{part}")
                        s = L.full(j)[:, 0:(t1 - t0) * 256].rearrange("p (t n) -> p t n", n=256)
                        L.free(a.activation(lf[:, t0:t1, h * 256:(h + 1) * 256], s, ACT.Exp, scale=-1.0), j)
                for part, t0, t1 in (("a", 0, 4), ("b", 4, 5)):
                    j = J(f"i{part}")
                    copy(iv[:, t0:t1, :], L.full(j)[:, 0:(t1 - t0) * 256].rearrange("p (t n) -> p t n", n=256), j)
                for t in range(2):
                    copy(qc[:, t, :], L.full(J(f"qc{t}"))[:, 0:NT], J(f"qc{t}"))
                for t in range(2):
                    L.free(a.activation(gbc[:, 2 + t, :], L.full(J(f"gc{t}"))[:, 0:NT], ACT.Silu), J(f"gc{t}"))
                L.need("conv_done")
                L.do(a.activation(cv, cv, ACT.Silu), "conv_silu")
                copy(koutb[:, :], L.full(J("kout"))[:, 0:P], J("kout"))
                copy(cachekT[:, :], L.full(J("ckt"))[:, 0:P], J("ckt"))

                def exps(x):
                    n, t = units[x]
                    w = window(n)[2]
                    sm = small[:, x % 2]
                    L.need("sm_in")
                    for f in range(2):
                        L.do(a.activation(a_s[x % 2][:, f, 0:w], a_s[x % 2][:, f, 0:w], ACT.Exp, bias=sm[:, 2 + f:3 + f],
                                          accum_out=sm[:, 4 + f:5 + f]))
                    L.do(a.activation(sm[:, 6:8], sm[:, 6:8], ACT.Exp), "sm_exp")

                exps(0)
                for x, (n, t) in enumerate(units):
                    if x + 1 < len(units):
                        exps(x + 1)
                    w = window(n)[2]
                    j = J(f"T{n}_{t}")
                    copy(a_pT[x % 2][:, :, 0:w], L.full(j).rearrange("p (f w) -> p f w", f=2)[:, :, 0:w], j)
                    j = J(f"O{n}_{t}")
                    copy(hT[:, t, n * P:(n + 1) * P], L.full(j)[:, 0:P], j)

                L.need("f_in")
                L.do(a.activation(lfd, lfd, ACT.Ln))
                L.do(a.activation(lf2, lf2, ACT.Ln), "f_ln")
                L.need("ab_in")
                L.do(a.activation(BETA, BETA, ACT.Exp, scale=-1.0))
                L.do(a.activation(SP, SP, ACT.Exp, scale=-1.0))
                L.do(a.activation(SP, SP, ACT.Ln, bias=1.0), "ab_exp")
                for t in range(4):
                    if t >= 2:
                        L.need("l2_ready")
                    j = J(f"l2{t}")
                    L.free(a.activation(rsb[t % 2], L.full(j)[:, 0:CVW], ACT.Ln, bias=eps[:, 1:2]), j)
                    L.do(a.activation(rsb[t % 2], rsb[t % 2], ACT.Exp, scale=-0.5), "l2_r")
                L.need("l2_ready", 2)
                for t in range(TT):
                    s = L.full(J(f"kv{t}"))
                    copy(ktok[:, t, :], s[:, 0:256])
                    copy(vtok[:, t, :], s[:, 256:512], J(f"kv{t}"))
                s = L.full(J("gate"))[:, 0:80].rearrange("p (d k n) -> p d k n", d=2, k=2)
                L.do(a.activation(EGC, s[:, :, 0], ACT.Exp))
                L.do(a.activation(EGL, s[:, :, 1], ACT.Exp), "v_exp")

                for n in range(5):
                    if n:
                        L.done(J(f"gs{n - 1}"))
                    s = L.full(J(f"grow{n}"))
                    L.do(a.activation(EG, s.rearrange("p (m i) -> p m i", m=8), ACT.Exp), "eg_ready")
                    L.need("dm_in")
                    L.do(a.activation(DM, DM, ACT.Exp), "dm_exp")
                    for v in range(1, LEV):
                        j = J(f"W{n}_{v}")
                        copy(Wb, L.full(j).rearrange("p (m i) -> p m i", m=8), j)
                    s = L.full(J(f"uw{n}"))
                    copy(u_b, s[:, 0:512].rearrange("p (m i) -> p m i", m=8))
                    copy(wT_b, s[:, 512:1024].rearrange("p (m i) -> p m i", m=4), J(f"uw{n}"))
                L.done(J("gs4"))
                for n in range(5):
                    if n:
                        L.done(J(f"hs{n - 1}"))
                    for d in range(2):
                        L.do(a.activation(KK[:, d], lf[:, chunk(d, n), d * 256:(d + 1) * 256], ACT.Exp),
                             "kk_exp" if d else None)
                    s = L.full(J(f"hk{n}"))
                    copy(KTt, s[:, 0:512].rearrange("p (m i) -> p m i", m=4))
                    L.free(a.activation(RV, s[:, 512:1024].rearrange("p (m i) -> p m i", m=2), ACT.Exp), J(f"hk{n}"))
                    for x in range(4):
                        if x >= 2:
                            L.done(J(f"P{n}_{x - 2}_1"))
                        j = J(f"E{n}_{x}")
                        L.free(a.activation(Eb[x % 2], L.full(j).rearrange("p (m i) -> p m i", m=8), ACT.Exp), j)
                for t in range(4):
                    if t >= 2:
                        L.need("o_ready")
                    j = J(f"rs{t}")
                    L.free(a.activation(orb[t % 2], L.full(j)[:, 0:NT], ACT.Ln, scale=1.0 / HD, bias=eps[:, 0:1]), j)
                    L.do(a.activation(orb[t % 2], orb[t % 2], ACT.Exp, scale=-0.5), "r_ready")
                L.need("o_ready", 2)

                def norm(i):
                    L.done(J(f"mean{i}"))
                    L.do(a.activation(hT[:, :, :], xT[:, :, :], ACT.Square), "sq_ready")
                    j = J(f"var{i}")
                    L.free(a.activation(rstd, L.full(j)[:, 0:NT], ACT.Ln, bias=eps[:, 0:1]), j)
                    L.do(a.activation(rstd, rstd, ACT.Exp, scale=-0.5), "rstd_ready")

                norm(1)
                if l % 2:
                    L.need("v_in")
                    L.do(a.activation(tq[:, 0], tq[:, 0], ACT.Exp), "v_exp")
                    for e in range(NE):
                        j = J(f"cb{e}")
                        copy(combB[:, e, :], L.full(j)[:, 0:NT], j)
                base = PS_BASE[l]

                def gate(i):
                    for t in range(2):
                        act.wait_ge(ps_free[2 + t], i * 3 + (base[2 + t] - 2))
                        act.wait_ge(ps_full[t], i * 3 + (base[t] + 1))
                        a.activation(gbuf[:, t], ps[:, t, 0:NT], ACT.Silu).then_inc(ps_free[t], 1)

                if l % 2 == 0:
                    with act.Fori(0, SLABS[0]) as s:
                        gate(s)
                else:
                    with act.Fori(0, NE) as e:
                        with act.Fori(0, ES) as s:
                            gate(e * ES + s)
                norm(2)
            for t in range(TT):
                copy(xin[:, t, :], L.full(f"yt{t}"), f"yt{t}")

        def route(L, v_, tt, ts, J):
            s = L.full(J("router"))[:, 0:40].rearrange("p (t e) -> p t e", t=TT)
            tt(lg, s, brr[:, :].unsqueeze(1).broadcast_to([P, TT, NE]), ALU.add, job=J("router"))
            for t in range(TT):
                L.do(v_.max(top[:, t], lg[:, t]))
            tt(tq[:, 0], top[:, :, 1], top[:, :, 0], ALU.subtract, to="v_in")
            le = lg.unsqueeze(3).broadcast_to([P, TT, NE, NE])
            lo = lg.unsqueeze(2).broadcast_to([P, TT, NE, NE])
            tt(ggt, lo, le, ALU.is_gt)
            tt(geq, lo, le, ALU.is_equal)
            tt(geq, geq, tie.rearrange("p (a b) -> p a b", a=NE).unsqueeze(1).broadcast_to([P, TT, NE, NE]), ALU.mult)
            tt(ggt, ggt, geq, ALU.add)
            L.do(v_.tensor_reduce(comb, ggt, AX_X, ALU.add))
            ts(first, comb, 0.0, ALU.is_equal)
            ts(comb, comb, 1.0, ALU.is_equal)
            L.need("v_exp")
            ts(tq[:, 1], tq[:, 0], 1.0, ALU.add)
            L.do(v_.reciprocal(tq[:, 1], tq[:, 1]))
            tt(tq[:, 2], tq[:, 0], tq[:, 1], ALU.mult)
            tt(first, first, tq[:, 1].unsqueeze(2).broadcast_to([P, TT, NE]), ALU.mult)
            tt(comb, comb, tq[:, 2].unsqueeze(2).broadcast_to([P, TT, NE]), ALU.mult)
            tt(comb, comb, first, ALU.add, to="comb_ready")

        @block.vector
        def _(dve):
            L = Lane(dve, "dve_chain")
            v_ = nc.vector

            def tt(o, x, y, op, to=None, job=None):
                ins = v_.tensor_tensor(o, x, y, op)
                L.free(ins, job) if job else L.do(ins, to)

            def ts(o, x, s1, op0, s2=None, op1=ALU.bypass, to=None, job=None):
                ins = v_.tensor_scalar(o, x, s1, s2, op0, op1)
                L.free(ins, job) if job else L.do(ins, to)

            def stt(o, x, s, y, op0, op1, to=None, job=None):
                ins = v_.scalar_tensor_tensor(out=o, in0=x, scalar=s, in1=y, op0=op0, op1=op1)
                L.free(ins, job) if job else L.do(ins, to)

            L.do(v_.memset(eps[:, 0:1], 1e-5))
            L.do(v_.memset(eps[:, 1:2], 1e-6))
            dve.wait_ge(sg["tab_in"], 16 * (1 + PAR_DMAS))
            tt(lbt[:, :], lbrow[:, 0], lbrow[:, 1], ALU.max)
            tt(lbrow[:, 0], lbrow[:, 0], lbt[:, :], ALU.subtract)
            tt(lbrow[:, 1], lbrow[:, 1], lbt[:, :], ALU.subtract, to="lb_in")
            L.need("lb_exp")
            tt(lbrow[:, 0], lbrow[:, 0], lbrow[:, 1], ALU.add)
            L.do(v_.reciprocal(lbt[:, :], lbrow[:, 0]))
            tt(lbt[:, :], lbt[:, :], lbrow[:, 1], ALU.mult)
            L.done("par")
            L.done(f"xt{TT - 1}")

            def modulate(shift, scale):
                for k in range(KT):
                    for g, a0, a1 in groups:
                        ts(hT[:, k, a0:a1], xT[:, k, a0:a1], modT[:, scale + k, g:g + 1], ALU.mult,
                           modT[:, shift + k, g:g + 1], ALU.add, to="h_ready" if (k, g) == (KT - 1, 1) else None)
                ts(xT[:, :, :], xT[:, :, :], ALPHA, ALU.mult)

            def norm(l, i):
                j = f"{l}.mean{i}"
                tt(xT[:, :, :], xT[:, :, :], L.full(j)[:, 0:NT].unsqueeze(1).broadcast_to([P, KT, NT]), ALU.subtract, job=j)
                L.need("rstd_ready")
                tt(xT[:, :, :], xT[:, :, :], rstd.unsqueeze(1).broadcast_to([P, KT, NT]), ALU.mult)
                for k in range(KT):
                    at = P + (l * 2 + i - 1) * KT + k
                    ts(xT[:, k, :], xT[:, k, :], par[:, at:at + 1], ALU.mult, par[:, 32 + at:33 + at], ALU.add,
                       to="xn_ready" if (l, i, k) == (DEPTH - 1, 2, KT - 1) else None)

            for l in range(DEPTH):
                J = lambda name: f"{l}.{name}"
                s = L.full(J("mod"))[:, 0:96].rearrange("p (t g) -> p t g", g=2)
                tt(modT[:, :, :], s, par[:, 48 * l:48 * l + 48].unsqueeze(2).broadcast_to([P, 48, 2]), ALU.add, job=J("mod"))
                ts(modT[:, 8:16, :], modT[:, 8:16, :], 1.0, ALU.add)
                ts(modT[:, 32:40, :], modT[:, 32:40, :], 1.0, ALU.add)
                modulate(0, 8)
                L.need("pad_zero")
                for t in range(6):
                    s = L.full(J(f"b{t}"))
                    L.do(v_.tensor_copy(pad[:, t, 2:2 + LAT], s[:, 0:LAT]))
                    L.free(v_.tensor_copy(pad[:, t, 4 + LAT:4 + NT], s[:, LAT:NT]), J(f"b{t}"))
                L.free(v_.tensor_copy(ba[:, :, :], L.full(J("ba"))[:, 0:80].rearrange("p (t n) -> p t n", t=TT)), J("ba"))
                for t in range(6):
                    for w in range(CONV):
                        at = P + 64 + (l * CONV + w) * 6 + t
                        if w == 0:
                            ts(cv[:, t, :], pad[:, t, 0:CVW], par[:, at:at + 1], ALU.mult)
                        else:
                            stt(cv[:, t, :], pad[:, t, w:w + CVW], par[:, at:at + 1], cv[:, t, :], ALU.mult, ALU.add,
                                to="conv_done" if (t, w) == (5, CONV - 1) else None)
                for t in range(5):
                    s = L.full(J(f"rot{t}"))
                    tt(mem(arena, 0, LAT), s[:, 0:LAT], sinT, ALU.mult, job=J(f"rot{t}"))
                    tt(qk[:, t, 0:LAT], qk[:, t, 0:LAT], cosT, ALU.mult)
                    tt(qk[:, t, 0:LAT], qk[:, t, 0:LAT], mem(arena, 0, LAT), ALU.add, to="rope_ready")

                def scores(x):
                    n, t = units[x]
                    _, _, w, _, m0 = window(n)
                    sm, S = small[:, x % 2], a_s[x % 2][:, :, 0:w]
                    j = J(f"S{n}_{t}")
                    s = L.full(j).rearrange("p (f w) -> p f w", f=2)[:, :, 0:w]
                    if n == 4:
                        ts(S, s, ATT_SCALE, ALU.mult, job=j)
                    else:
                        stt(S, s, ATT_SCALE, am[:, m0:m0 + w].unsqueeze(1).broadcast_to([P, 2, w]), ALU.mult, ALU.add, job=j)
                    L.do(v_.tensor_reduce(sm[:, 0:2], S, AX_X, ALU.max))
                    snk = sink[:, l * 8 + t:l * 8 + t + 5:4]
                    tt(sm[:, 0:2], sm[:, 0:2], snk, ALU.max)
                    ts(sm[:, 2:4], sm[:, 0:2], -1.0, ALU.mult)
                    tt(sm[:, 6:8], snk, sm[:, 0:2], ALU.subtract, to="sm_in")

                def divide(x):
                    w = window(units[x][0])[2]
                    sm, S = small[:, x % 2], a_s[x % 2]
                    L.need("sm_exp")
                    tt(sm[:, 8:10], sm[:, 4:6], sm[:, 6:8], ALU.add)
                    L.do(v_.reciprocal(sm[:, 10:12], sm[:, 8:10]))
                    for f in range(2):
                        ts(S[:, f, 0:w], S[:, f, 0:w], sm[:, 10 + f:11 + f], ALU.mult, to="prob_ready" if f else None)

                scores(0)
                for x in range(len(units)):
                    if x + 1 < len(units):
                        scores(x + 1)
                    divide(x)
                L.done(J("O4_3"))
                ts(lfd, lfd, 1.0, ALU.add)
                L.do(v_.reciprocal(lfd, lfd))
                if l:
                    lbb = lbt[:, :].unsqueeze(1).broadcast_to([P, TT, 512])
                    tmp = lf2.rearrange("p (t n) -> p t n", t=TT)
                    tt(tmp, lf, lbb, ALU.mult)
                    tt(lf, lf, tmp, ALU.subtract)
                    tt(lf, lf, lbb, ALU.add)
                ts(lf2, lfd, 1e-30, ALU.max, 2.0 ** -60, ALU.min)
                ts(lf2, lf2, 2.0 ** 60, ALU.mult)
                ts(lfd, lfd, 2.0 ** -60, ALU.max, to="f_in")
                zb = ba[:, :, 0:8].rearrange("p t (d h) -> p d t h", d=2)
                za = ba[:, :, 8:16].rearrange("p t (d h) -> p d t h", d=2)

                def by_head(v):
                    return v[:, l * 8:l * 8 + 8].rearrange("p (d h) -> p d h", d=2).unsqueeze(2).broadcast_to([P, 2, TT, 4])

                def four(v):
                    return v.rearrange("p d (t h) -> p d t h", t=TT)

                L.do(v_.tensor_copy(four(BETA), zb))
                tt(four(ZA), za, by_head(dtb), ALU.add)
                stt(SP, ZA, -1.0, ZA, ALU.mult, ALU.max, to="ab_in")
                L.need("f_ln")
                tt(lfd, lfd, lf2, ALU.add, to="lf_ready")
                L.need("ab_exp")
                ts(BETA, BETA, 1.0, ALU.add)
                L.do(v_.reciprocal(BETA, BETA))
                stt(ZA, ZA, 0.0, SP, ALU.max, ALU.add)
                tt(four(ZA), four(ZA), by_head(alog), ALU.mult)
                ts(LA, ZA, -1.0, ALU.mult, to="la_ready")
                for t in range(4):
                    L.need("l2_r")
                    stt(cv[:, t, :], cv[:, t, :], HD ** -0.5 if t < 2 else 1.0, rsb[t % 2], ALU.mult, ALU.mult, to="l2_ready")
                s = L.full(J("gate"))[:, 0:80].rearrange("p (d k n) -> p d k n", d=2, k=2)
                L.need("v_exp")
                L.free(v_.tensor_copy(GC, s[:, :, 0]), J("gate"))
                tt(BG, BETA, EGC, ALU.mult, to="g_ready")

                def update(S, slot, weight, job, n, tile):
                    for d in range(2):
                        cc = chunk(d, n) * P
                        tt(hT[:, tile:tile + 2, cc:cc + P], hT[:, tile:tile + 2, cc:cc + P],
                           slot[:, d * 256:d * 256 + 256].rearrange("p (r i) -> p r i", r=2), ALU.add)
                    if n == 3:
                        L.free(v_.memset(S[:, :, :], 0.0), job)
                        return
                    for f in range(2):
                        r0, r1 = f * HD, (f + 1) * HD
                        for x in range(4):
                            stt(S[r0:r1, x, r0:r1], S[r0:r1, x, r0:r1], weight(f, x)[r0:r1],
                                slot[r0:r1, 512 + x * HD:512 + (x + 1) * HD], ALU.mult, ALU.add,
                                job=job if (f, x) == (1, 3) else None)

                L.need("o_zero")
                for n in range(5):
                    s = L.full(J(f"grow{n}")).rearrange("p (m i) -> p m i", m=8)
                    L.need("eg_ready")
                    for d in range(2):
                        gg = gate_of(GC, d, chunk(d, n)).unsqueeze(3).broadcast_to([P, 2, 2, P])
                        tt(per_dir(DM, d), per_dir(s, d), gg, ALU.subtract, job=J(f"grow{n}") if d else None)
                    ts(DM, DM, 0.0, ALU.min, to="dm_in")
                    L.need("dm_exp")
                    for f in range(2):
                        tt(per_half(DM, f), per_half(DM, f), inc.unsqueeze(2).broadcast_to([P, 2, 2, P]), ALU.mult)
                    eight = lambda j: L.full(J(j)).rearrange("p (m i) -> p m i", m=8)
                    tt(LT, DM, eight(f"brow{n}"), ALU.mult, job=J(f"brow{n}"))
                    tt(LT, LT, eight(f"G{n}"), ALU.mult, job=J(f"G{n}"))
                    tt(AT, DM, eight(f"KQ{n}"), ALU.mult, job=J(f"KQ{n}"))
                    idb = ident.unsqueeze(1).broadcast_to([P, 8, P])
                    tt(T_, idb, eight(f"W{n}_0"), ALU.subtract, job=J(f"W{n}_0"))
                    tt(Tt, idb, CS[0], ALU.subtract, to="t_ready")
                    for v in range(1, LEV):
                        if v < LEV - 1:
                            tt(T_, T_, eight(f"T{n}__{v}"), ALU.subtract, job=J(f"T{n}__{v}"))
                        tt(Tt, Tt, eight(f"TT{n}_{v}"), ALU.subtract, job=J(f"TT{n}_{v}"))
                    L.done(J(f"uw{n}"))
                    s = L.full(J(f"vn{n}"))
                    tt(vnew, u_b, s[:, 0:512].rearrange("p (m i) -> p m i", m=8), ALU.subtract, job=J(f"vn{n}"))
                    update(SG, L.full(J(f"gs{n}")), lambda f, x: EG[:, f * 4 + x, last_row(x // 2):last_row(x // 2) + 1],
                           J(f"gs{n}"), n, 4)
                for n in range(5):
                    L.need("kk_exp")
                    ts(KK, KK, -1.0, ALU.mult, 1.0, ALU.add, to="kk_ready")

                    def weigh_q(x):
                        d, r = divmod(x, 2)
                        cc = chunk(d, n) * P
                        L.done(J(f"E{n}_{x}"))
                        q = qc[:, r, cc:cc + P]
                        tt(QE[x % 2], Eb[x % 2][:, 0:7, :], q.unsqueeze(1).broadcast_to([P, 7, P]), ALU.mult)
                        tt(QB[:, x], Eb[x % 2][:, 7, :], q, ALU.mult)
                        L.do(v_.tensor_copy(ebl[:, x:x + 1], Eb[x % 2][:, 7, last_row(d):last_row(d) + 1]), "qe_ready")

                    weigh_q(0)
                    for x in range(4):
                        if x < 3:
                            weigh_q(x + 1)
                        for f in range(2):
                            j = J(f"P{n}_{x}_{f}")
                            tt(PM, L.full(j).rearrange("p (m i) -> p m i", m=8), mk[:, x // 2], ALU.mult, job=j)
                            L.do(v_.tensor_reduce(AH[:, f * 4 + x], PM.rearrange("p m i -> p i m"), AX_X, ALU.add),
                                 "ah_ready" if (x, f) == (3, 1) else None)
                    update(SH, L.full(J(f"hs{n}")), lambda f, x: ebl[:, x:x + 1], J(f"hs{n}"), n, 6)
                for t in range(4):
                    L.need("r_ready")
                    at = 2 * P + (t // 2) * 2 + l
                    stt(hT[:, 4 + t, :], hT[:, 4 + t, :], par[:, at:at + 1], orb[t % 2], ALU.mult, ALU.mult)
                    tt(hT[:, 4 + t, :], hT[:, 4 + t, :], gbc[:, t, :], ALU.mult, to="o_ready")
                for m in range(KT):
                    s = L.full(J(f"wo{m}"))
                    for g, a0, a1 in groups:
                        stt(xT[:, m, a0:a1], s[:, a0:a1], modT[:, 16 + m, g:g + 1], xT[:, m, a0:a1], ALU.mult, ALU.add,
                            job=J(f"wo{m}") if g else None)
                norm(l, 1)
                modulate(24, 32)
                L.do(v_.memset(yacc, 0.0))
                if l % 2:
                    route(L, v_, tt, ts, J)
                base = PS_BASE[l]

                def slab(i):
                    for t in range(2):
                        dve.wait_ge(ps_full[2 + t], i * 3 + (base[2 + t] + 1))
                        if l % 2:
                            dve.wait_ge(sg["g_comb"], i * 2 + (t + 1))
                        else:
                            dve.wait_ge(ps_free[t], i * 3 + (base[t] + 1))
                        v_.tensor_tensor(abuf[:, t], gbuf[:, t], ps[:, 2 + t, 0:NT], ALU.mult).then_inc(ps_free[2 + t], 1)
                    for m in range(KT):
                        b = m % 4
                        dve.wait_ge(ps_full[b], i * 3 + (base[b] + 2 + m // 4))
                        v_.tensor_tensor(yacc[:, m], yacc[:, m], ps[:, b, 0:NT], ALU.add).then_inc(ps_free[b], 1)

                if l % 2 == 0:
                    with dve.Fori(0, SLABS[0]) as s:
                        slab(s)
                else:
                    with dve.Fori(0, NE) as e:
                        with dve.Fori(0, ES) as s:
                            slab(e * ES + s)
                for b in range(4):
                    dve.wait_ge(ps_free[b], base[b] + 3 * SLABS[l])
                for m in range(KT):
                    for g, a0, a1 in groups:
                        stt(xT[:, m, a0:a1], yacc[:, m, a0:a1], modT[:, 40 + m, g:g + 1], xT[:, m, a0:a1], ALU.mult, ALU.add,
                            to="z_ready" if (m, g) == (KT - 1, 1) else None)
                norm(l, 2)

        @block.tensor
        def _(pe):
            L = Lane(pe, None)
            mm_, tr_ = nc.tensor.matmul, nc.tensor.transpose

            def open_(job):
                slot, turn = PS[job]
                if turn:
                    pe.wait_ge(ps_free[slot], turn)
                return ps[:, slot]

            def close(ins, job):
                ins.then_inc(ps_full[PS[job][0]], 1)

            def piece(name):
                slot, turn = WP[name]
                pe.wait_ge(w_full[slot], 64 * (turn + 1))
                return wpiece(slot)

            def mm(o, w, x, first=True, last=True):
                return mm_(o, w, x, start=first, stop=last, skip_group_check=True)

            def wide(s, w, x, first, last):
                mm(s[:, 0:LAT], w, x[:, 0:LAT], first, last)
                return mm(s[:, LAT:NT], w, x[:, LAT:NT], first, last)

            def project(name, job, lo, src=None):
                w = piece(name)
                s = open_(job)
                for k in range(KT):
                    ins = wide(s, w[:, k, lo:lo + P], hT[:, k], k == 0, k == KT - 1)
                close(ins, job)

            pe.wait_ge(sg["tab_in"], 16 * (1 + PAR_DMAS))
            pe.wait_ge(sg["x_in"], 16 * TT)
            for t in range(TT):
                s = open_(f"xt{t}")
                for k in range(KT):
                    ins = tr_(s[:, k * P:(k + 1) * P], xin[:, t, k * P:(k + 1) * P], ident)
                close(ins, f"xt{t}")
            s = open_("par")
            for k in range(3):
                ins = tr_(s[:, k * P:(k + 1) * P], rows[:, k, :], ident)
            close(ins, "par")

            for l in range(DEPTH):
                J = lambda name: f"{l}.{name}"
                if l == 0:
                    L.need("siluc_ready")
                s = open_(J("mod"))
                cvec = siluc[:, :].rearrange("p (g k) -> p k g", g=2)
                for i in range(24):
                    w = piece(J(f"mod{i}"))
                    for t in range(2):
                        o = 2 * (2 * i + t)
                        for k in range(KT):
                            ins = mm(s[:, o:o + 2], w[:, k, t * P:(t + 1) * P], cvec[:, k], k == 0, k == KT - 1)
                    if i < 23:
                        ins.then_inc(sg["mod_used"], 1)
                close(ins, J("mod"))
                L.need("h_ready")
                for t in range(4):
                    project(J(f"qa{t // 2}"), J(f"q{t}"), (t % 2) * P)
                project(J("kv"), J("ka"), 0)
                w = piece(J("kv"))

                def tokens(job, w, cols, tiles):
                    s = open_(job)
                    lo, hi = cols
                    n = hi - lo
                    for i, t in enumerate(tiles):
                        for k in range(KT):
                            ins = mm(s[:, i * n:(i + 1) * n], hT[:, k, t * P:(t + 1) * P], w[:, k, lo:hi], k == 0, k == KT - 1)
                    close(ins, job)

                tokens(J("va"), w, (P, 256), range(TT))
                for t in range(6):
                    project(J(f"b{t // 2}"), J(f"b{t}"), (t % 2) * P)
                for t in range(2):
                    project(J("gb"), J(f"gb{t}"), t * P)
                slot = WP[J("ba")][0]
                piece(J("ba"))
                tokens(J("ba"), wpiece(slot, 16), (0, 16), range(TT))
                for p_ in ("f0", "f1", "i"):
                    w = piece(J(p_))
                    tokens(J(p_ + "a"), w, (0, 256), range(4))
                    tokens(J(p_ + "b"), w, (0, 256), range(4, 5))
                for p_ in ("qc", "gc"):
                    for t in range(2):
                        project(J(p_), J(f"{p_}{t}"), t * P)
                L.done(J("ka"))
                s = open_(J("kout"))
                close(tr_(s[:, 0:P], qk[:, 4, LAT:NT], ident), J("kout"))
                pe.wait_ge(sg["cache_in"], 32 * (l + 1))
                s = open_(J("ckt"))
                close(tr_(s[:, 0:P], cachek[:, :], ident), J("ckt"))
                for t in range(5):
                    s = open_(J(f"rot{t}"))
                    close(mm(s[:, 0:LAT], rot, qk[:, t, 0:LAT]), J(f"rot{t}"))
                L.need("rope_ready", 5)
                L.done(J("ckt"))
                L.done(J("va"))

                def score(x):
                    n, t = units[x]
                    cache_at, band_at, w, tok, _ = window(n)
                    s = open_(J(f"S{n}_{t}"))
                    for f in range(2):
                        r0, r1 = f * HD, (f + 1) * HD
                        q = qk[r0:r1, t, n * P:(n + 1) * P]
                        band = w - (P if cache_at is not None else 0)
                        ins = mm(s[:, f * 512 + band_at:f * 512 + band_at + band], q, qk[r0:r1, 4, tok:tok + band])
                        if cache_at is not None:
                            ins = mm(s[:, f * 512 + cache_at:f * 512 + cache_at + P], q, cachekT[r0:r1, :])
                    close(ins, J(f"S{n}_{t}"))

                score(0)
                for x, (n, t) in enumerate(units):
                    if x + 1 < len(units):
                        score(x + 1)
                    cache_at, band_at, w, tok, _ = window(n)
                    L.need("prob_ready")
                    s = open_(J(f"T{n}_{t}"))
                    for f in range(2):
                        for b in range(w // P):
                            ins = tr_(s[:, f * 512 + b * P:f * 512 + (b + 1) * P], a_s[x % 2][:, f, b * P:(b + 1) * P], ident)
                    close(ins, J(f"T{n}_{t}"))
                    s = open_(J(f"O{n}_{t}"))
                    L.done(J(f"T{n}_{t}"))
                    for f in range(2):
                        for b in range(w // P):
                            if cache_at is not None and b * P == cache_at:
                                vals = cachev[:, f * HD:(f + 1) * HD]
                            else:
                                vals = va[:, (tok + b * P - band_at) // P, f * HD:(f + 1) * HD]
                            ins = mm(s[f * HD:(f + 1) * HD, 0:P], vals, a_pT[x % 2][:, f, b * P:(b + 1) * P],
                                     b == 0, b == w // P - 1)
                    close(ins, J(f"O{n}_{t}"))

                L.need("l2_sq")
                for t in range(4):
                    s = open_(J(f"l2{t}"))
                    mm(s[:, 0:512], blk, sqb[:, t, 0:512])
                    close(mm(s[:, 512:CVW], blk, sqb[:, t, 512:CVW]), J(f"l2{t}"))
                L.need("l2_ready", 4)
                for t in range(TT):
                    s = open_(J(f"kv{t}"))
                    cc = cv_col(t)
                    for i in range(4):
                        ins = tr_(s[:, i * P:(i + 1) * P], cv[:, 2 + i, cc:cc + P], ident)
                    close(ins, J(f"kv{t}"))
                L.need("la_ready")
                s = open_(J("gate"))
                for d in range(2):
                    mm(s[:, d * 40:d * 40 + 20], inc[:, d], LA[:, d])
                    ins = mm(s[:, d * 40 + 20:d * 40 + 40], rev[:, d], LA[:, d])
                close(ins, J("gate"))
                if l == 0:
                    pe.wait_ge(sg["state_in"], 64)
                else:
                    pe.wait_ge(sg["state_in"], 128)

                problems = [(f, d, r) for f in range(2) for d in range(2) for r in range(2)]
                L.done(J("gate"))
                for n in range(5):
                    def gate_row(v, d, r, f):
                        at = 4 * chunk(d, n) + 2 * r + f
                        return v[:, d, at:at + 1].broadcast_to([P, P])

                    def at(m):
                        return slice(m * P, (m + 1) * P)

                    s = open_(J(f"grow{n}"))
                    for m, (f, d, r) in enumerate(problems):
                        ins = mm(s[:, at(m)], gate_row(LA, d, r, f), inc[:, d])
                    close(ins, J(f"grow{n}"))
                    s = open_(J(f"brow{n}"))
                    for m, (f, d, r) in enumerate(problems):
                        ins = mm(s[:, at(m)], gate_row(BETA, d, r, f), ident)
                    close(ins, J(f"brow{n}"))
                    for job, first_tile in ((J(f"G{n}"), 2), (J(f"KQ{n}"), 0)):
                        s = open_(job)
                        for m, (f, d, r) in enumerate(problems):
                            cc = cv_col(chunk(d, n))
                            r0, r1 = f * HD, (f + 1) * HD
                            ins = mm(s[:, at(m)], cv[r0:r1, 2 + r, cc:cc + P], cv[r0:r1, first_tile + r, cc:cc + P])
                        close(ins, job)
                    L.need("cs_ready")
                    s = open_(J(f"W{n}_0"))
                    for m in range(8):
                        ins = mm(s[:, at(m)], CS[0][:, m], ident)
                    close(ins, J(f"W{n}_0"))
                    for v in range(1, LEV):
                        L.need("cs_ready")
                        if v == 1:
                            L.need("t_ready")
                        else:
                            L.done(J(f"TT{n}_{v - 1}"))
                        s = open_(J(f"W{n}_{v}"))
                        for m in range(8):
                            ins = mm(s[:, at(m)], CS[v % 2][:, m], T_[:, m])
                        close(ins, J(f"W{n}_{v}"))
                        L.done(J(f"W{n}_{v}"))
                        if v < LEV - 1:
                            s = open_(J(f"T{n}__{v}"))
                            for m in range(8):
                                ins = mm(s[:, at(m)], Tt[:, m], Wb[:, m])
                            close(ins, J(f"T{n}__{v}"))
                        s = open_(J(f"TT{n}_{v}"))
                        for m in range(8):
                            ins = mm(s[:, at(m)], Wb[:, m], Tt[:, m])
                        close(ins, J(f"TT{n}_{v}"))
                    L.need("vk_ready")
                    L.done(J(f"TT{n}_{LEV - 1}"))
                    s = open_(J(f"uw{n}"))
                    for m, (f, d, r) in enumerate(problems):
                        mm(s[:, m * HD:(m + 1) * HD], Tt[:, m], vb[:, m])
                        x = 2 * d + r
                        ins = mm(s[f * HD:(f + 1) * HD, 512 + x * P:512 + (x + 1) * P], kbg[:, m], Tt[:, m])
                    close(ins, J(f"uw{n}"))
                    L.done(J(f"uw{n}"))
                    s = open_(J(f"vn{n}"))
                    if n:
                        L.done(J(f"gs{n - 1}"))
                    for x in range(4):
                        for f in range(2):
                            m = f * 4 + x
                            ins = mm(s[:, m * HD:(m + 1) * HD], wT_b[:, x], SG[:, x, f * HD:(f + 1) * HD])
                    close(ins, J(f"vn{n}"))
                    L.done(J(f"vn{n}"))
                    L.done(J(f"KQ{n}"))
                    s = open_(J(f"gs{n}"))
                    for x in range(4):
                        mm(s[:, at(x)], SG[:, x], qg[:, x], True, False)
                        for f in range(2):
                            mm(s[f * HD:(f + 1) * HD, at(x)], vnew[:, f * 4 + x], AT[:, f * 4 + x], False, True)
                    for x in range(4):
                        for f in range(2):
                            ins = mm(s[f * HD:(f + 1) * HD, 512 + x * HD:512 + (x + 1) * HD], kd[:, f * 4 + x],
                                     vnew[:, f * 4 + x])
                    close(ins, J(f"gs{n}"))

                for n in range(5):
                    L.need("kk_ready")
                    s = open_(J(f"hk{n}"))
                    for x in range(4):
                        tr_(s[:, x * P:(x + 1) * P], KK[:, x // 2, (x % 2) * P:(x % 2 + 1) * P], ident)
                    for d in range(2):
                        ins = mm(s[:, 512 + d * 256:512 + (d + 1) * 256], rev[:, d], lf[:, chunk(d, n), d * 256:(d + 1) * 256])
                    close(ins, J(f"hk{n}"))

                    def exponents(x):
                        d, r = divmod(x, 2)
                        s = open_(J(f"E{n}_{x}"))
                        for b in range(2):
                            ins = mm(s[:, b * 512:(b + 1) * 512], lf[:, chunk(d, n), x * P:(x + 1) * P], hg[:, d, 4 * b:4 * b + 4])
                        close(ins, J(f"E{n}_{x}"))

                    exponents(0)
                    for x in range(4):
                        if x < 3:
                            exponents(x + 1)
                        d, r = divmod(x, 2)
                        L.need("qe_ready")
                        L.need("ke_ready")
                        for f in range(2):
                            r0, r1 = f * HD, (f + 1) * HD
                            s = open_(J(f"P{n}_{x}_{f}"))
                            for v in range(LEV):
                                mm(s[:, v * P:(v + 1) * P], KE[x % 2][r0:r1, v], QE[x % 2][r0:r1, v])
                            cc = chunk(d, n) * P
                            ins = mm(s[:, 7 * P:8 * P], KTt[r0:r1, x], qc[r0:r1, r, cc:cc + P])
                            close(ins, J(f"P{n}_{x}_{f}"))
                    L.need("ah_ready")
                    L.need("kd_ready")
                    if n:
                        L.done(J(f"hs{n - 1}"))
                    s = open_(J(f"hs{n}"))
                    for x in range(4):
                        d, r = divmod(x, 2)
                        mm(s[:, x * P:(x + 1) * P], SH[:, x], QB[:, x], True, False)
                        for f in range(2):
                            h = 2 * r + f
                            mm(s[f * HD:(f + 1) * HD, x * P:(x + 1) * P], iv[:, chunk(d, n), h * HD:(h + 1) * HD],
                               AH[:, f * 4 + x], False, True)
                    for x in range(4):
                        d, r = divmod(x, 2)
                        for f in range(2):
                            h = 2 * r + f
                            ins = mm(s[f * HD:(f + 1) * HD, 512 + x * HD:512 + (x + 1) * HD],
                                     KD[:, d, h * HD:(h + 1) * HD], iv[:, chunk(d, n), h * HD:(h + 1) * HD])
                    close(ins, J(f"hs{n}"))

                L.need("o_sq")
                for t in range(4):
                    s = open_(J(f"rs{t}"))
                    close(wide(s, blk, osq[:, t], True, True), J(f"rs{t}"))
                L.need("o_ready", 4)
                for m in range(KT):
                    project(J(f"wo{m // 2}"), J(f"wo{m}"), (m % 2) * P)

                def over_features(job, x):
                    s = open_(job)
                    for k in range(KT):
                        ins = wide(s, mean, x[:, k], k == 0, k == KT - 1)
                    close(ins, job)

                L.done(J(f"wo{KT - 1}"))
                over_features(J("mean1"), xT)
                L.need("sq_ready")
                over_features(J("var1"), hT)
                L.need("h_ready")
                if l % 2:
                    s = open_(J("router"))
                    for t in range(TT):
                        for k in range(KT):
                            ins = mm(s[:, t * NE:(t + 1) * NE], hT[:, k, t * P:(t + 1) * P], wr[:, k], k == 0, k == KT - 1)
                    close(ins, J("router"))
                    L.need("comb_ready")
                    for e in range(NE):
                        s = open_(J(f"cb{e}"))
                        for t in range(TT):
                            ins = mm(s[:, t * P:(t + 1) * P], comb[:, t, e:e + 1].broadcast_to([P, P]), ident)
                        close(ins, J(f"cb{e}"))
                base, wbase = PS_BASE[l], WP_BASE[l]

                def slab(i):
                    for j, slot in enumerate((0, 0, 1, 1)):
                        if j % 2 == 0:
                            pe.wait_ge(w_full[slot], i * 64 + 64 * (wbase[slot] + 1))
                        pe.wait_ge(ps_free[j], i * 3 + base[j])
                        w = wpiece(slot)
                        for k in range(KT):
                            ins = wide(ps[:, j], w[:, k, (j % 2) * P:(j % 2 + 1) * P], hT[:, k], k == 0, k == KT - 1)
                        ins.then_inc(ps_full[j], 1)
                    pe.wait_ge(w_full[2], i * 64 + 64 * (wbase[2] + 1))
                    w2 = wbuf[:, 2, :].rearrange("p (t n) -> p t n", t=2)
                    for m in range(3):
                        pe.wait_ge(ps_free[m], i * 3 + (base[m] + 1))
                        if m == 0:
                            pe.wait_ge(ps_free[2], i * 3 + (base[2] + 1))
                        wide(ps[:, m], w2[:, 0, m * P:(m + 1) * P], abuf[:, 0], True, False)
                    pe.wait_ge(ps_free[3], i * 3 + (base[3] + 1))
                    for m in range(KT):
                        b = m % 4
                        if m >= 3:
                            pe.wait_ge(ps_free[b], i * 3 + (base[b] + 1 + m // 4))
                            wide(ps[:, b], w2[:, 0, m * P:(m + 1) * P], abuf[:, 0], True, False)
                        ins = wide(ps[:, b], w2[:, 1, m * P:(m + 1) * P], abuf[:, 1], False, True)
                        ins.then_inc(ps_full[b], 1)

                if l % 2 == 0:
                    with pe.Fori(0, SLABS[0]) as s:
                        slab(s)
                else:
                    with pe.Fori(0, NE) as e:
                        with pe.Fori(0, ES) as s:
                            slab(e * ES + s)
                L.need("z_ready")
                over_features(J("mean2"), xT)
                L.need("sq_ready")
                over_features(J("var2"), hT)
            L.need("xn_ready")
            for t in range(TT):
                s = open_(f"yt{t}")
                for k in range(KT):
                    ins = tr_(s[:, k * P:(k + 1) * P], xT[:, k, t * P:(t + 1) * P], ident)
                close(ins, f"yt{t}")


PAR_DMAS = 16
_INS = ["x_prompt", "x_sample", "cache_k", "cache_v", "state_gdn", "state_hgrn", "c", "c_ctx", "w_mod", "b_mod", "w_in",
        "conv_w", "attn_sink", "gdn_a_log", "gdn_dt_bias", "gdn_norm_w", "hgrn_lb", "hgrn_norm_w", "w_out", "ln_g", "ln_b",
        "ffn_w1", "ffn_w3", "ffn_w2", "moe_router", "moe_router_b", "moe_w1", "moe_w3", "moe_w2"]
_OUTS = [(1, CTX, D), (1, LAT, D), (1, DEPTH, CTX, 2, HD), (1, DEPTH, CTX, 2, HD), (1, DEPTH, 2, 4, HD, HD),
         (1, DEPTH, 2, 4, HD, HD)]


def kernel(**inputs):
    import concourse.bacc as bacc
    from concourse.bass_utils import run_bass_kernel_spmd

    nc = bacc.Bacc("TRN2", target_bir_lowering=False, num_devices=1)
    arrays, args = {}, []
    for name in _INS + ["table"]:
        a = np.ascontiguousarray(constant_table() if name == "table" else inputs[name])
        arrays[f"in_{name}"] = a
        args.append(nc.dram_tensor(f"in_{name}", a.shape, mybir.dt.from_np(a.dtype), kind="ExternalInput").ap())
    for i, shape in enumerate(_OUTS):
        args.append(nc.dram_tensor(f"out_{i}", shape, F32, kind="ExternalOutput").ap())
    backbone_kernel(nc, *args)
    r = run_bass_kernel_spmd(nc, [arrays], core_ids=[0])
    return tuple(r.results[0][f"out_{i}"] for i in range(len(_OUTS)))
```

```python
from contextlib import ExitStack

import numpy as np

import concourse.bass as bass
from concourse import mybir

ALU = mybir.AluOpType
ACT = mybir.ActivationFunctionType
F32 = mybir.dt.float32
F16 = mybir.dt.float16
AX_X = mybir.AxisListType.X

P = 128
D = 1024
KT = D // P
LAT = 512
CTX = 128
NT = LAT + CTX
TT = NT // P
DEPTH = 2
HD = 64
D_IN = 3088
D_FF = 2816
NE = 8
EFF = 1024
CONV = 5
PADW = NT + 6
CVW = NT + 2
SLAB = 256
LEV = 7
SLOTS = 4
ALPHA = (2.0 * DEPTH) ** 0.25
ATT_SCALE = HD ** -0.5
WS = 1024.0
IWS = 1.0 / WS
OFF_BA, OFF_F, OFF_I, OFF_QC, OFF_GC, OFF_GB, OFF_B, OFF_KV = 1792, 1808, 2320, 2576, 2832, 1536, 768, 512

_WIDTH = [("ident", P), ("mean", 1), ("blk", P), ("rot", P), ("hg", 2 * 8 * P),
          ("mk", 2 * 8 * P), ("rev", 2 * P), ("am", 5 * P), ("tie", 64), ("cos", LAT), ("sin", LAT)]
CONST_AT = {}
_at = 0
for _n, _w in _WIDTH:
    CONST_AT[_n] = (_at, _w)
    _at += _w
NCONST = _at
NRES = CONST_AT["cos"][0]


def constant_table():
    t = np.zeros((P, NCONST), np.float32)

    def put(name, a):
        o, w = CONST_AT[name]
        t[:, o:o + w] = np.asarray(a, np.float32).reshape(P, w)

    put("ident", np.eye(P))
    put("mean", np.full((P, 1), 1.0 / D))
    i = np.arange(P)
    put("blk", (i[:, None] // HD) == (i[None, :] // HD))
    rot = np.zeros((P, P))
    for m in range(P):
        if m % 32 < 16:
            rot[m + 16, m] = -1.0
        else:
            rot[m - 16, m] = 1.0
    put("rot", rot)
    inv = np.float32(10000.0) ** (-np.arange(16, dtype=np.float32) * np.float32(2.0) / np.float32(32))
    tok = np.arange(LAT)
    pos = np.where(((i % HD) // 32 == 0)[:, None], (tok // 64)[None, :], (tok % 64)[None, :]).astype(np.float32)
    ang = (pos * inv[i % 16][:, None]).astype(np.float32)
    put("cos", np.cos(ang))
    put("sin", np.sin(ang))
    a, b = i[:, None], i[None, :]
    hg = np.zeros((P, 8, P))
    mk = np.zeros((P, 8, P))
    for lev in range(LEV):
        s = 1 << lev
        mid = (b // (2 * s)) * 2 * s + s - 1
        right = (b % (2 * s)) >= s
        hg[:, lev] = np.where(right, (a > mid) & (a <= b), (a > b) & (a <= mid))
        mk[:, lev] = (a // (2 * s) == b // (2 * s)) & ((a % (2 * s)) < s) & right
    hg[:, 7] = a <= b
    mk[:, 7] = a == b
    put("hg", np.stack([hg, hg[::-1, :, ::-1]], 1))
    put("mk", np.stack([mk, mk[::-1, :, ::-1]], 1))
    put("rev", np.stack([a > b, a < b], 1))
    zero = np.zeros((P, P))
    before = np.where(b >= a, 0.0, -1e30)
    after = np.where(b <= a, 0.0, -1e30)
    put("am", np.stack([zero, before, zero, after, zero], 1))
    e = np.arange(8)
    put("tie", np.broadcast_to((e[None, :] < e[:, None]).reshape(1, 64), (P, 64)))
    return t


def chunk(d, n):
    return 4 if n == 4 else (n if d == 0 else 3 - n)


def cv_col(c):
    return c * P + (2 if c == 4 else 0)


def mod_pieces(x):
    return (2 * x, 2 * x + 1)


def mod_piece(i):
    return (0, i + 8) if i < 16 else (1, i - 16)


def mod_job(x):
    if x.startswith("*mp"):
        l, i = mod_piece(int(x[3:]))
        return f"{l}.mp{i}"
    l, i = mod_piece(4 * int(x[3:]))
    return f"{l}.mt{i // 4}"


def psum_plan():
    names = [f"xt{t}" for t in range(TT)] + ["par"]
    for i in range(8):
        names += [f"0.mp{i}"] + ([f"0.mt{i // 4}"] if i % 4 == 3 else [])
    loops = {}
    for l in range(DEPTH):
        j = [f"q{t}" for t in range(4)] + ["ka", "va"] + [f"b{t}" for t in range(6)]
        j += ["gb0", "gb1", "ba", "f0a", "f0b", "f1a", "f1b", "ia", "ib", "qc0", "qc1", "gc0", "gc1", "kout", "ckt"]
        j += [f"rot{t}" for t in range(5)]
        units = [f"{n}_{t}" for n in range(5) for t in range(4)]
        j += ["S" + units[0], "S" + units[1]]
        for x in range(len(units)):
            if x + 2 < len(units):
                j.append("S" + units[x + 2])
            j.append("T" + units[x])
            if l == 0:
                j += ["*mp" + str(i) for i in mod_pieces(x)]
            if x:
                j.append("O" + units[x - 1])
            if l == 0 and x % 2:
                j.append("*mt" + str(x // 2))
        j.append("O" + units[-1])
        j += [f"l2{t}" for t in range(4)] + [f"kv{t}" for t in range(TT)] + ["gate"]
        for n in range(5):
            j += [f"grow{n}", f"brow{n}", f"G{n}", f"KQ{n}"]
            for v in range(LEV):
                j += [f"W{n}_{v}"] + ([f"T{n}__{v}"] if 0 < v < LEV - 1 else []) + ([f"TT{n}_{v}"] if v else [])
            j += [f"uw{n}", f"vn{n}", f"gs{n}"]
        for n in range(5):
            j += [f"hk{n}"]
            for x in range(5):
                if x < 4:
                    j.append(f"E{n}_{x}")
                if x >= 1:
                    j += [f"P{n}_{x - 1}_0", f"P{n}_{x - 1}_1"]
            j += [f"hs{n}"]
        j += [f"rs{t}" for t in range(4)] + [f"wo{m}" for m in range(KT)] + ["mean1", "var1"]
        if l % 2:
            j += ["router"] + [f"cb{e}" for e in range(NE)]
        names += [mod_job(x) if x[0] == "*" else f"{l}.{x}" for x in j]
        while len(names) % SLOTS:
            names.append(None)
        loops[l] = len(names)
        names += [f"{l}.ffn"] * (12 * (NE * EFF // SLAB if l % 2 else D_FF // SLAB))
        names += [f"{l}.mean2", f"{l}.var2"]
    names += [f"yt{t}" for t in range(TT)]
    plan, turns, base = {}, [0] * SLOTS, {}
    for n, name in enumerate(names):
        for l, at in loops.items():
            if n == at:
                base[l] = list(turns)
        if name is None:
            continue
        plan[name] = (n % SLOTS, turns[n % SLOTS])
        turns[n % SLOTS] += 1
    return plan, base


def weight_plan():
    names, loops = [], {}
    for l in range(DEPTH):
        j = ["qa0", "qa1", "kv", "b0", "b1", "b2", "gb", "ba", "f0", "f1", "i", "qc", "gc"]
        if l == 0:
            names += [f"0.mod{i}" for i in range(8)]
        names += [f"{l}.{x}" for x in j]
        if l == 0:
            for i in range(40):
                names.append("%d.mod%d" % mod_piece(i))
        names += [f"{l}.wo{i}" for i in range(4)]
        while len(names) % 3:
            names.append(None)
        loops[l] = len(names)
        names += [f"{l}.ffn"] * (3 * (NE * EFF // SLAB if l % 2 else D_FF // SLAB))
    plan, turns, base, split, split_base, order = {}, [0] * 3, {}, {}, {}, []
    for n, name in enumerate(names):
        for l, at in loops.items():
            if n == at:
                base[l] = list(turns)
                split_base[l] = len(order)
        if name is None:
            continue
        plan[name] = (n % 3, turns[n % 3])
        turns[n % 3] += 1
        if "mod" not in name:
            if not name.endswith("ffn"):
                split[name] = len(order)
            order.append(name)
    return plan, base, [n for n in names if n], split, split_base


def release(l, what):
    if what.startswith("wo"):
        return f"{l}.wo{2 * int(what[2]) + 1}"
    return f"{l}." + {"qa0": "q1", "qa1": "q3", "kv": "va", "b0": "b1", "b1": "b3", "b2": "b5",
                      "gb": "gb1", "ba": "ba", "f0": "f0b", "f1": "f1b", "i": "ib", "qc": "qc1", "gc": "gc1"}[what]


def backbone_kernel(nc, x_prompt, x_sample, cache_k, cache_v, state_gdn, state_hgrn, c, c_ctx, w_mod, b_mod, w_in,
                    conv_w, attn_sink, gdn_a_log, gdn_dt_bias, gdn_norm_w, hgrn_lb, hgrn_norm_w, w_out, ln_g, ln_b,
                    ffn_w1, ffn_w3, ffn_w2, moe_router, moe_router_b, moe_w1, moe_w3, moe_w2, table,
                    y_prompt, y_sample, new_k, new_v, new_sg, new_sh):
    PS, PS_BASE = psum_plan()
    WP, WP_BASE, WNAMES, SPLIT, SPLIT_BASE = weight_plan()
    SLABS = [D_FF // SLAB, NE * EFF // SLAB]
    A_BASE = [0, 2 * SLABS[0]]
    ES = EFF // SLAB
    ctx = ExitStack()
    with ctx:
        def sb(name, shape):
            return ctx.enter_context(nc.sbuf_tensor(name, shape, F32))

        def sem(name):
            return ctx.enter_context(nc.semaphore(name))

        const = sb("const", [P, NRES])
        xT = sb("xT", [P, KT, NT])
        hTf = sb("hT", [P, KT * NT])
        arena = sb("arena", [P, KT * NT + 5 * NT])
        extra = sb("extra", [P, 2560])
        wbuf = sb("wbuf", [P, 3, 2048])
        PADN, CVN = 6 * PADW, 6 * CVW
        mix = sb("mix", [P, PADN + CVN + 6 * NT + TT * 768])
        va = sb("va", [P, TT, P])
        cachek = sb("cachek", [P, P])
        cachekT = sb("cachekT", [P, P])
        cachev = sb("cachev", [P, P])
        koutb = sb("koutb", [P, P])
        ba = sb("ba", [P, TT, 16])
        gates = sb("gates", [P, 8, 2, 20])
        SG = sb("SG", [P, 4, P])
        SH = sb("SH", [P, 4, P])
        modT = sb("modT", [P, DEPTH, 48, 2])
        par = sb("par", [P, 3 * P])
        sink = sb("sink", [P, DEPTH * 8])
        alog = sb("alog", [P, DEPTH * 8])
        dtb = sb("dtb", [P, DEPTH * 8])
        lbt = sb("lbt", [P, 512])
        siluc = sb("siluc", [P, 16])
        small = sb("small", [P, 3, 16])
        eps = sb("eps", [P, 2])
        wr = sb("wr", [P, KT, NE])
        brr = sb("brr", [P, NE])
        ebl = sb("ebl", [P, 4])
        modrow = sb("modrow", [P, 1024])
        revb = sb("revb", [P, P])
        wr16 = sb("wr16", [P, KT * NE])
        ps = ctx.enter_context(nc.psum_tensor("ps", [P, SLOTS, 1024], F32))

        def mem(t, at, *shape):
            v = t[:, at:at + int(np.prod(shape))]
            if len(shape) == 2:
                return v.rearrange("p (a b) -> p a b", a=shape[0])
            if len(shape) == 3:
                return v.rearrange("p (a b c) -> p a b c", a=shape[0], b=shape[1])
            return v

        def cst(name, *shape):
            o, w = CONST_AT[name]
            return mem(const, o, *(shape + (w // int(np.prod(shape)),)))

        def parts(v, *shape):
            h = v.bitcast(F16)
            n = int(np.prod(shape))
            return [h[:, i * n:(i + 1) * n].rearrange("p (a b) -> p a b", a=shape[0]) for i in range(2)]

        ident, blk, rot, am, tie = (cst(n) for n in ("ident", "blk", "rot", "am", "tie"))
        hT = mem(hTf, 0, KT, NT)
        h2 = parts(hTf[:, :], KT, NT)
        htmp = mem(extra, 1408, NT)
        wr2 = parts(wr16[:, :], KT, NE)
        mean = cst("mean").broadcast_to([P, P])
        hg, mk, rev = cst("hg", 2, 8), cst("mk", 2, 8), cst("rev", 2)
        inc = hg[:, :, 7]

        pad = mem(mix, 0, 6, PADW)
        ktok = mem(mix, 0, TT, 256)
        vtok = mem(mix, TT * 256, TT, 256)
        kd = mem(mix, 2 * TT * 256, 8, HD)
        qg = mem(mix, 2 * TT * 256 + 512, 4, P)
        cv = mem(mix, PADN, 6, CVW)
        u_b = mem(mix, PADN + 4 * CVW, 8, HD)
        wT_b = mem(mix, PADN + 4 * CVW + 512, 4, P)
        gbc = mem(mix, PADN + CVN, 4, NT)
        qc = mem(mix, PADN + CVN + 4 * NT, 2, NT)
        lf = mem(mix, PADN + CVN + 6 * NT, TT, 512)
        lfd = mem(mix, PADN + CVN + 6 * NT, TT * 512)
        iv = mem(mix, PADN + CVN + 6 * NT + TT * 512, TT, 256)
        combB = mem(mix, 0, NE, NT)
        gbuf = mem(mix, NE * NT, 2, NT)
        a2 = parts(mem(mix, NE * NT + 2 * NT, 2 * NT), 2, NT)
        rstd = mem(mix, NE * NT + 4 * NT, NT)
        rt = NE * NT + 5 * NT
        lg, top, comb, first = (mem(mix, rt + 40 * i, TT, NE) for i in range(4))
        ggt, geq = (mem(mix, rt + 160 + 320 * i, TT, NE, NE) for i in range(2))
        tq = mem(mix, rt + 800, 3, TT)

        SPLIT_IN = [mem(arena, 2048 * i, 2048) for i in range(2)]
        SPLIT_OUT = [mem(mix, 2048 * i, 2048) for i in range(2)]
        FFN_AT = PADN + CVN + 6 * NT + TT * 768 - 3 * 2048
        SPLIT_FFN = [mem(mix, FFN_AT + 2048 * i, 2048) for i in range(3)]
        assert rt + 815 <= FFN_AT
        o2 = parts(mem(arena, 3200, KT * NT), KT, NT)
        cosT, sinT = mem(arena, 4096, LAT), mem(arena, 4096 + LAT, LAT)
        rtmp = mem(extra, 0, LAT)

        yacc = mem(arena, 0, KT, NT)
        xin = mem(arena, 0, TT, D)
        qk = mem(arena, KT * NT, 5, NT)
        a_s = [mem(arena, 1024 * i, 2, 512) for i in (0, 1, 4)]
        a_pT = [mem(arena, 2048 + 1024 * i, 2, 512) for i in range(2)]
        lf2 = mem(arena, 0, TT * 512)
        sqb = mem(arena, 0, 4, CVW)
        rsb = [mem(arena, 4 * CVW + CVW * i, CVW) for i in range(2)]
        osq = mem(arena, 0, 4, NT)
        orb = [mem(arena, 4 * NT, NT), mem(extra, 0, NT)]
        EG, DM, LT, T_, Tt, Wb, AT = [mem(arena, 1024 * i, 8, P) for i in range(7)]
        vb = mem(arena, 7168, 8, HD)
        kbg = mem(arena, 7680, 8, HD)
        CS = [mem(extra, 1024 * i, 8, P) for i in range(2)]
        vnew = mem(extra, 2048, 8, HD)
        Eb = [mem(arena, 1024 * i, 8, P) for i in range(2)]
        QE = [mem(arena, 2048 + 896 * i, 7, P) for i in range(2)]
        KE = [mem(arena, 3840 + 896 * i, 7, P) for i in range(2)]
        PM = mem(arena, 5632, 8, P)
        AH = mem(arena, 6656, 8, P)
        QB = mem(arena, 7680, 4, P)
        KK = mem(extra, 0, 2, 256)
        KTt = mem(extra, 512, 4, P)
        KD = mem(extra, 1024, 2, 256)
        RV = mem(extra, 1536, 2, 256)
        lp = parts(mem(extra, 2048, 512), 2, 256)
        hg16 = modrow[:, :].bitcast(F16).rearrange("p (d v i) -> p d v i", d=2, v=8)
        rev16 = revb[:, :].bitcast(F16).rearrange("p (d i) -> p d i", d=2)
        lbrow = mem(extra, 0, 2, 512)
        rows = mem(extra, 1024, 3, P)
        LA, BETA, ZA, SP, BG, EGL, GC, EGC = (gates[:, i] for i in range(8))

        w_full = [sem(f"w_full{i}") for i in range(3)]
        ps_full = [sem(f"ps_full{i}") for i in range(SLOTS)]
        ps_free = [sem(f"ps_free{i}") for i in range(SLOTS)]
        sg = {n: sem(n) for n in (
            "act_chain dve_chain pool_chain "
            "tab_in x_in rope_in cache_in state_in out_done yt_out rows_clear s_clear w_hi w_lo wr_hi wr_ready "
            "w_scaled mod_ready x_ready hi_ready oa_hi oa_lo om_hi om_lo a_hi a_lo "
            "siluc_ready lb_in lb_exp h_ready pad_zero conv_done conv_silu rope_ready sm_in sm_exp prob_ready "
            "f_in f_ln lf_ready l2_sq l2_r l2_ready ab_in ab_exp la_ready g_ready "
            "eg_ready dm_in dm_exp vk_ready cs_ready t_ready "
            "hg_ready lp_hi lp_lo kk_exp kk_ready kd_ready qe_ready ke_ready ah_ready o_zero o_sq r_ready o_ready "
            "z_ready sq_ready rstd_ready xn_ready v_in v_exp comb_ready g_comb").split()}
        OUTS = 16 * 6

        block = ctx.enter_context(nc.Block())

        class Lane:

            def __init__(self, eng, chain):
                self.eng, self.chain, self.made, self.took = eng, chain, {}, {}

            def do(self, ins, to=None):
                s = to or self.chain
                self.made[s] = self.made.get(s, 0) + 1
                ins.then_inc(sg[s], 1)
                self.eng.wait_ge(sg[s], self.made[s])

            def need(self, s, n=1):
                self.took[s] = self.took.get(s, 0) + n
                self.eng.wait_ge(sg[s], self.took[s])

            def full(self, job):
                slot, turn = PS[job]
                self.eng.wait_ge(ps_full[slot], turn + 1)
                return ps[:, slot]

            def free(self, ins, job):
                slot, turn = PS[job]
                ins.then_inc(ps_free[slot], 1)
                self.eng.wait_ge(ps_free[slot], turn + 1)

            def done(self, job):
                slot, turn = PS[job]
                self.eng.wait_ge(ps_free[slot], turn + 1)

        def wpiece(slot, n=256):
            return wbuf[:, slot, 0:8 * n].rearrange("p (k n) -> p k n", k=KT)

        IN_PIECES = ["qa0", "qa1", "kv", "b0", "b1", "b2", "gb", "ba", "f0", "f1", "i", "qc", "gc"]
        OUT_PIECES = ["wo0", "wo1", "wo2", "wo3"]

        def split_of(what):
            if what in IN_PIECES:
                i = IN_PIECES.index(what)
                return SPLIT_IN[i % 2], (16 if what == "ba" else 256), (IN_PIECES[i - 2] if i >= 2 else None)
            i = OUT_PIECES.index(what)
            return SPLIT_OUT[i % 2], 256, (OUT_PIECES[i - 2] if i >= 2 else None)

        def split_parts(what):
            region, n, _ = split_of(what)
            return parts(region[:, 0:KT * n], KT, n)

        def heads_of(state, f):
            return state.rearrange("d (r f) k v -> f k (d r) v", f=2)[f]

        def diag(S, f):
            return S[f * HD:(f + 1) * HD, :, f * HD:(f + 1) * HD]

        def per_half(v, f):
            return v[:, 4 * f:4 * f + 4].rearrange("p (d r) i -> p d r i", d=2)

        def per_dir(v, d):
            return v.rearrange("p (f e r) i -> p f e r i", f=2, e=2)[:, :, d]

        def gate_of(v, d, c):
            return v[:, d, 4 * c:4 * c + 4].rearrange("p (r f) -> p f r", r=2)

        def last_row(d):
            return P - 1 if d == 0 else 0

        xo = [(x_sample, t * P) for t in range(4)] + [(x_prompt, 0)]
        yo = [(y_sample, t * P) for t in range(4)] + [(y_prompt, 0)]
        groups = ((0, 0, LAT), (1, LAT, NT))

        def window(n):
            if n == 4:
                return None, 0, P, LAT, None
            if n == 0:
                return 2 * P, 0, 3 * P, 0, 2 * P
            return 0, P, (4 if n < 3 else 3) * P, (n - 1) * P, 0

        units = [(n, t) for n in range(5) for t in range(4)]

        @block.sync
        def _(sp):
            sp.dma_start(const[:, :], table[:, 0:NRES]).then_inc(sg["tab_in"], 16)
            for t in range(TT):
                src, r = xo[t]
                sp.dma_start(xin[:, t, :], src[0, r:r + P, :]).then_inc(sg["x_in"], 16)
            last = [None] * 3

            def freed(slot):
                if last[slot] is None:
                    return
                l, what = last[slot]
                if what == "ffn":
                    sp.wait_ge(sg["w_lo"], SPLIT_BASE[l] + 3 * (SLABS[l] - 1) + slot + 1)
                elif what.startswith("mod"):
                    bank, turn = PS[f"{l}.mp{what[3:]}"]
                    sp.wait_ge(ps_full[bank], turn + 1)
                else:
                    sp.wait_ge(sg["w_lo"], SPLIT[f"{l}.{what}"] + 1)

            def fetch(name):
                slot, turn = WP[name]
                l, what = int(name[0]), name[2:]
                freed(slot)
                last[slot] = (l, what)
                dst = wpiece(slot)

                def cols(w, off, n):
                    return w[l].rearrange("(k p) n -> p k n", p=P)[:, :, off:off + n]

                if what.startswith("mod"):
                    parts = [(dst, cols(w_mod, int(what[3:]) * 256, 256))]
                elif what.startswith("qa"):
                    v = dst.rearrange("p k (t g j) -> p k t g j", t=2, g=2)
                    parts = [(v[:, :, t, g, :], cols(w_in, (g * 4 + int(what[2]) * 2 + t) * HD, HD))
                             for t in range(2) for g in range(2)]
                elif what.startswith("wo"):
                    src = w_out[l][:, int(what[2]) * 256:int(what[2]) * 256 + 256]
                    parts = [(dst[g * HD:(g + 1) * HD, 0:4, :],
                              src[g * 256:(g + 1) * 256, :].rearrange("(t j) n -> j t n", j=HD)) for g in range(2)]
                    parts += [(dst[:, k:k + 2, :], src[k * P:(k + 2) * P, :].rearrange("(k p) n -> p k n", p=P))
                              for k in (4, 6)]
                elif what == "ba":
                    parts = [(wpiece(slot, 16), cols(w_in, OFF_BA, 16))]
                else:
                    off = {"kv": OFF_KV, "b0": OFF_B, "b1": OFF_B + 256, "b2": OFF_B + 512, "gb": OFF_GB, "f0": OFF_F,
                           "f1": OFF_F + 256, "i": OFF_I, "qc": OFF_QC, "gc": OFF_GC}[what]
                    parts = [(dst, cols(w_in, off, 256))]
                for o, i in parts:
                    sp.dma_start(o, i).then_inc(w_full[slot], 64 // len(parts))

            def slab(l, w1, w3, w2, i):
                for slot, src, dst in ((0, w1, wpiece(0)), (1, w3, wpiece(1)),
                                       (2, w2, wbuf[:, 2, :].rearrange("p (t n) -> p t n", t=2))):
                    sp.wait_ge(sg["w_lo"], i * 3 + (SPLIT_BASE[l] + slot - 2))
                    sp.dma_start(dst, src).then_inc(w_full[slot], 64)

            for l in range(DEPTH):
                lo = 0 if l == 0 else WNAMES.index("1.qa0")
                for name in WNAMES[lo:WNAMES.index(f"{l}.wo3") + 1]:
                    fetch(name)
                    if name == f"{l}.kv":
                        if l:
                            sp.wait_ge(sg["out_done"], OUTS * l)
                        else:
                            sp.wait_ge(sg["s_clear"], 1)
                        for S, st in ((SG, state_gdn), (SH, state_hgrn)):
                            for f in range(2):
                                sp.dma_start(diag(S, f), heads_of(st[0, l], f)).then_inc(sg["state_in"], 16)
                for slot in range(3):
                    freed(slot)
                    last[slot] = (l, "ffn")
                if l % 2 == 0:
                    w1 = ffn_w1[0].rearrange("(k p) (s n) -> p s k n", p=P, n=SLAB)
                    w3 = ffn_w3[0].rearrange("(k p) (s n) -> p s k n", p=P, n=SLAB)
                    w2 = ffn_w2[0].rearrange("(s t p) n -> p s t n", p=P, t=2)
                    with sp.Fori(0, SLABS[0]) as s:
                        slab(l, w1[:, s], w3[:, s], w2[:, s], s)
                else:
                    w1 = moe_w1[0].rearrange("e (k p) (s n) -> p e s k n", p=P, n=SLAB)
                    w3 = moe_w3[0].rearrange("e (k p) (s n) -> p e s k n", p=P, n=SLAB)
                    w2 = moe_w2[0].rearrange("e (s t p) n -> p e s t n", p=P, t=2)
                    with sp.Fori(0, NE) as e:
                        with sp.Fori(0, ES) as s:
                            slab(l, w1[:, e, s], w3[:, e, s], w2[:, e, s], e * ES + s)
            L = Lane(sp, None)
            for t in range(TT):
                L.done(f"yt{t}")
                dst, r = yo[t]
                sp.dma_start(dst[0, r:r + P, :], xin[:, t, :]).then_inc(sg["yt_out"], 16)
            sp.wait_ge(sg["yt_out"], 16 * TT)
            sp.wait_ge(sg["out_done"], OUTS * DEPTH)

        @block.gpsimd
        def _(pool):
            L = Lane(pool, "pool_chain")
            g = nc.gpsimd
            L.do(g.memset(rows[:, :, :], 0.0), "rows_clear")
            L.do(g.memset(SG[:, :, :], 0.0))
            L.do(g.memset(SH[:, :, :], 0.0), "s_clear")
            L.need("wr_hi")
            L.do(g.tensor_tensor(wr2[1], wr[:, :, :], wr2[0], ALU.subtract), "wr_ready")

            def lower(l, what):
                L.need("w_hi")
                _, n, _ = split_of(what)
                L.do(g.tensor_tensor(split_parts(what)[1], wpiece(WP[f"{l}.{what}"][0], n), split_parts(what)[0],
                                     ALU.subtract), "w_lo")

            for l in range(DEPTH):
                lower(l, "qa0")
                lower(l, "qa1")
                L.need("h_ready", KT)
                if l:
                    pool.wait_ge(sg["out_done"], OUTS * l)
                pool.dma_start(mem(arena, 4096, 2 * LAT), table[:, NRES:NCONST]).then_inc(sg["rope_in"], 16)
                pool.dma_start(cachek[:, :], cache_k[0, l].rearrange("t g d -> t (g d)")).then_inc(sg["cache_in"], 16)
                pool.dma_start(cachev[:, :], cache_v[0, l].rearrange("t g d -> t (g d)")).then_inc(sg["cache_in"], 16)
                L.do(g.memset(mem(mix, 0, PADN), 0.0), "pad_zero")
                for what in IN_PIECES[2:]:
                    lower(l, what)
                L.done(f"{l}.kout")
                pool.dma_start(new_k[0, l].rearrange("t g d -> t (g d)"), koutb[:, :]).then_inc(sg["out_done"], 16)
                pool.dma_start(new_v[0, l].rearrange("t g d -> t (g d)"), va[:, 4, :]).then_inc(sg["out_done"], 16)
                L.full(f"{l}.gc1")
                L.do(g.memset(hT[:, 4:8, :], 0.0), "o_zero")
                L.need("conv_silu")
                L.need("lf_ready")
                L.do(g.tensor_tensor(sqb, cv[:, 0:4, :], cv[:, 0:4, :], ALU.mult), "l2_sq")
                L.need("g_ready")
                L.done(f"{l}.kv4")
                for n in range(5):
                    if n:
                        L.done(f"{l}.gs{n - 1}")
                    for d in range(2):
                        cc = chunk(d, n)
                        for dst, src, sc in ((vb, vtok, BETA), (kbg, ktok, BG), (kd, ktok, EGL)):
                            L.do(g.tensor_tensor(per_dir(dst, d), src[:, cc].rearrange("p (r f j) -> p f r j", r=2, f=2),
                                                 gate_of(sc, d, cc).unsqueeze(3).broadcast_to([P, 2, 2, HD]), ALU.mult))
                    L.need("eg_ready")
                    for f in range(2):
                        r0, r1 = f * HD, (f + 1) * HD
                        for d in range(2):
                            cc = cv_col(chunk(d, n))
                            L.do(g.tensor_tensor(qg[r0:r1, 2 * d:2 * d + 2, :], cv[r0:r1, 0:2, cc:cc + P],
                                                 EG[r0:r1, f * 4 + 2 * d:f * 4 + 2 * d + 2, :], ALU.mult),
                                 "vk_ready" if f and d else None)
                    L.done(f"{l}.G{n}")
                    for v in range(LEV):
                        if v == 2:
                            L.need("t_ready")
                        if v > 2:
                            L.done(f"{l}.TT{n}_{v - 2}")
                        for f in range(2):
                            L.do(g.tensor_tensor(per_half(CS[v % 2], f), per_half(LT, f),
                                                 mk[:, :, v].unsqueeze(2).broadcast_to([P, 2, 2, P]), ALU.mult),
                                 "cs_ready" if f else None)
                L.done(f"{l}.gs4")

                def lower_gates(n):
                    L.need("lp_hi")
                    for d in range(2):
                        L.do(g.tensor_tensor(lp[1][:, d], lf[:, chunk(d, n), d * 256:(d + 1) * 256], lp[0][:, d],
                                             ALU.subtract), "lp_lo" if d else None)

                lower_gates(0)
                for n in range(5):
                    L.done(f"{l}.hk{n}")
                    L.do(g.tensor_tensor(KD, KK, RV, ALU.mult), "kd_ready")
                    for x in range(4):
                        L.done(f"{l}.E{n}_{x}")
                        if x >= 2:
                            L.done(f"{l}.P{n}_{x - 2}_1")
                        L.do(g.tensor_tensor(KE[x % 2], Eb[x % 2][:, 0:7, :],
                                             KTt[:, x].unsqueeze(1).broadcast_to([P, 7, P]), ALU.mult), "ke_ready")
                    if n < 4:
                        lower_gates(n + 1)
                    L.done(f"{l}.hs{n}")
                for S, dst in ((SG, new_sg), (SH, new_sh)):
                    for f in range(2):
                        pool.dma_start(heads_of(dst[0, l], f), diag(S, f)).then_inc(sg["out_done"], 16)
                L.do(g.tensor_tensor(osq, hT[:, 4:8, :], hT[:, 4:8, :], ALU.mult), "o_sq")
                L.need("oa_hi")
                L.do(g.tensor_tensor(o2[1][:, 0:4, :], hT[:, 0:4, :], o2[0][:, 0:4, :], ALU.subtract), "oa_lo")
                for what in OUT_PIECES:
                    lower(l, what)
                base, sbase = PS_BASE[l], SPLIT_BASE[l]

                def slab(i, e, i0):
                    for j in range(3):
                        pool.wait_ge(sg["w_hi"], i * 3 + (sbase + j + 1 + 3 * i0))
                        v = parts(SPLIT_FFN[j], KT, 256)
                        g.tensor_tensor(v[1], wpiece(j), v[0], ALU.subtract).then_inc(sg["w_lo"], 1)
                    if l % 2:
                        for t in range(2):
                            pool.wait_ge(ps_free[t], i * 3 + (base[t] + 1 + 3 * i0))
                            g.tensor_tensor(gbuf[:, t], gbuf[:, t], combB[:, e], ALU.mult).then_inc(sg["g_comb"], 1)
                    for t in range(2):
                        pool.wait_ge(sg["a_hi"], i * 2 + (A_BASE[l] + t + 1 + 2 * i0))
                        g.tensor_tensor(a2[1][:, t], gbuf[:, t], a2[0][:, t], ALU.subtract).then_inc(sg["a_lo"], 1)

                for e in range(NE if l % 2 else 1):
                    with pool.Fori(0, ES if l % 2 else SLABS[0]) as s:
                        slab(s, e, ES * e)
                L.made["w_lo"] = sbase + 3 * SLABS[l]
                L.took["w_hi"] = sbase + 3 * SLABS[l]

        @block.scalar
        def _(act):
            L = Lane(act, "act_chain")
            a = nc.scalar

            def copy(dst, src, job=None, scale=1.0):
                ins = a.activation(dst, src, ACT.Copy, scale=scale)
                L.free(ins, job) if job else L.do(ins)

            def upper(l, what):
                slot, turn = WP[f"{l}.{what}"]
                _, n, before = split_of(what)
                act.wait_ge(w_full[slot], 64 * (turn + 1))
                L.do(a.activation(wpiece(slot, n), wpiece(slot, n), ACT.Copy, scale=WS))
                if before:
                    L.full(release(l, before))
                L.do(a.activation(split_parts(what)[0], wpiece(slot, n), ACT.Copy), "w_hi")

            def upper_h(l, shift, scale, each):
                for k in range(KT):
                    if each:
                        L.need("x_ready")
                    for g_, a0, a1 in groups:
                        L.do(a.activation(h2[0][:, k, a0:a1], xT[:, k, a0:a1], ACT.Identity,
                                          scale=modT[:, l, scale + k, g_:g_ + 1], bias=modT[:, l, shift + k, g_:g_ + 1]),
                             "hi_ready" if g_ else None)

            def mod_row(l, i):
                j = f"{l}.mp{i}"
                copy(modrow[0:2, (i % 4) * 256:(i % 4 + 1) * 256], L.full(j)[0:2, 0:256], j)

            L.need("rows_clear")
            par_in = [(rows[0:96, 0, :], b_mod.rearrange("l (t p) -> (l t) p", p=P)),
                      (rows[96:104, 0, :], c[0].rearrange("(k p) -> k p", p=P)),
                      (rows[104:112, 0, :], c_ctx.rearrange("(k p) -> k p", p=P)),
                      (rows[0:32, 1, :], ln_g.rearrange("l i (k p) -> (l i k) p", p=P)),
                      (rows[32:64, 1, :], ln_b.rearrange("l i (k p) -> (l i k) p", p=P)),
                      (rows[64:124, 1, :], conv_w.rearrange("l w (t p) -> (l w t) p", p=P))]
            par_in += [(rows[2 * i:2 * i + 2, 2, f * HD:(f + 1) * HD], w)
                       for i, w in enumerate((gdn_norm_w, hgrn_norm_w)) for f in range(2)]
            par_in += [(sink[:, :], attn_sink.rearrange("l h -> (l h)").partition_broadcast(P)),
                       (alog[:, :], gdn_a_log.rearrange("l d h -> (l d h)").partition_broadcast(P)),
                       (dtb[:, :], gdn_dt_bias.rearrange("l d h -> (l d h)").partition_broadcast(P)),
                       (lbrow.rearrange("p l n -> p (l n)"), hgrn_lb.rearrange("l d n -> (l d n)").partition_broadcast(P)),
                       (brr[:, :], moe_router_b[0].partition_broadcast(P)),
                       (wr[:, :, :], moe_router[0].rearrange("(k p) e -> p k e", p=P))]
            assert len(par_in) == PAR_DMAS
            for o, i in par_in:
                act.dma_start(o, i).then_inc(sg["tab_in"], 16)
            for t in range(TT):
                s = L.full(f"xt{t}")
                copy(xT[:, :, t * P:(t + 1) * P], s.rearrange("p (k i) -> p k i", k=KT), f"xt{t}")
            copy(par[:, :], L.full("par")[:, 0:3 * P], "par")
            L.do(a.activation(siluc[:, :], par[:, 96:112], ACT.Silu), "siluc_ready")
            L.need("lb_in")
            L.do(a.activation(lbrow, lbrow, ACT.Exp))
            L.do(a.activation(alog[:, :], alog[:, :], ACT.Exp), "lb_exp")
            L.do(a.activation(wr[:, :, :], wr[:, :, :], ACT.Copy, scale=WS))
            L.do(a.activation(wr2[0], wr[:, :, :], ACT.Copy), "wr_hi")
            for i in range(8):
                mod_row(0, i)

            for l in range(DEPTH):
                J = lambda name: f"{l}.{name}"
                upper(l, "qa0")
                upper(l, "qa1")
                if l == 0:
                    L.need("mod_ready")
                upper_h(l, 0, 8, l > 0)
                if l:
                    act.wait_ge(sg["out_done"], OUTS * l)
                for t in range(4):
                    if t == 2:
                        upper(l, "kv")
                    copy(qk[:, t, :], L.full(J(f"q{t}"))[:, 0:NT], J(f"q{t}"), IWS)
                upper(l, "b0")
                copy(qk[:, 4, :], L.full(J("ka"))[:, 0:NT], J("ka"), IWS)
                copy(va[:, :, :], L.full(J("va"))[:, 0:NT].rearrange("p (t n) -> p t n", t=TT), J("va"), IWS)
                for what in ("b1", "b2", "gb", "ba"):
                    upper(l, what)
                for t in range(2):
                    L.free(a.activation(gbc[:, t, :], L.full(J(f"gb{t}"))[:, 0:NT], ACT.Silu, scale=IWS), J(f"gb{t}"))
                upper(l, "f0")
                upper(l, "f1")
                for h in range(2):
                    for part, t0, t1 in (("a", 0, 4), ("b", 4, 5)):
                        j = J(f"f{h}{part}")
                        s = L.full(j)[:, 0:(t1 - t0) * 256].rearrange("p (t n) -> p t n", n=256)
                        L.free(a.activation(lf[:, t0:t1, h * 256:(h + 1) * 256], s, ACT.Exp, scale=-IWS), j)
                    upper(l, ("i", "qc")[h])
                for part, t0, t1 in (("a", 0, 4), ("b", 4, 5)):
                    j = J(f"i{part}")
                    copy(iv[:, t0:t1, :], L.full(j)[:, 0:(t1 - t0) * 256].rearrange("p (t n) -> p t n", n=256), j, IWS)
                upper(l, "gc")
                for t in range(2):
                    copy(qc[:, t, :], L.full(J(f"qc{t}"))[:, 0:NT], J(f"qc{t}"), IWS)
                for t in range(2):
                    L.free(a.activation(gbc[:, 2 + t, :], L.full(J(f"gc{t}"))[:, 0:NT], ACT.Silu, scale=IWS), J(f"gc{t}"))
                L.need("conv_done")
                L.do(a.activation(cv, cv, ACT.Silu), "conv_silu")
                copy(koutb[:, :], L.full(J("kout"))[:, 0:P], J("kout"))
                copy(cachekT[:, :], L.full(J("ckt"))[:, 0:P], J("ckt"))

                def exps(x):
                    n, t = units[x]
                    w = window(n)[2]
                    sm = small[:, x % 3]
                    L.need("sm_in")
                    for f in range(2):
                        L.do(a.activation(a_s[x % 3][:, f, 0:w], a_s[x % 3][:, f, 0:w], ACT.Exp, bias=sm[:, 2 + f:3 + f],
                                          accum_out=sm[:, 4 + f:5 + f]))
                    L.do(a.activation(sm[:, 6:8], sm[:, 6:8], ACT.Exp), "sm_exp")

                def output(x):
                    n, t = units[x]
                    j = J(f"O{n}_{t}")
                    copy(hT[:, t, n * P:(n + 1) * P], L.full(j)[:, 0:P], j)

                exps(0)
                exps(1)
                for x, (n, t) in enumerate(units):
                    w = window(n)[2]
                    j = J(f"T{n}_{t}")
                    copy(a_pT[x % 2][:, :, 0:w], L.full(j).rearrange("p (f w) -> p f w", f=2)[:, :, 0:w], j)
                    if l == 0:
                        for i in mod_pieces(x):
                            mod_row(*mod_piece(i))
                    if x:
                        output(x - 1)
                    if x + 2 < len(units):
                        exps(x + 2)
                output(len(units) - 1)
                if l == 0:
                    L.full(f"1.mt{5}")
                    L.do(a.activation(hg16, hg, ACT.Copy))
                    L.do(a.activation(rev16, rev, ACT.Copy), "hg_ready")

                L.need("f_in")
                L.do(a.activation(lfd, lfd, ACT.Ln))
                L.do(a.activation(lf2, lf2, ACT.Ln), "f_ln")
                L.need("ab_in")
                L.do(a.activation(BETA, BETA, ACT.Exp, scale=-1.0))
                L.do(a.activation(SP, SP, ACT.Exp, scale=-1.0))
                L.do(a.activation(SP, SP, ACT.Ln, bias=1.0), "ab_exp")
                for t in range(4):
                    if t >= 2:
                        L.need("l2_ready")
                    j = J(f"l2{t}")
                    L.free(a.activation(rsb[t % 2], L.full(j)[:, 0:CVW], ACT.Ln, bias=eps[:, 1:2]), j)
                    L.do(a.activation(rsb[t % 2], rsb[t % 2], ACT.Exp, scale=-0.5), "l2_r")
                L.need("l2_ready", 2)
                for t in range(TT):
                    s = L.full(J(f"kv{t}"))
                    copy(ktok[:, t, :], s[:, 0:256])
                    copy(vtok[:, t, :], s[:, 256:512], J(f"kv{t}"))
                s = L.full(J("gate"))[:, 0:80].rearrange("p (d k n) -> p d k n", d=2, k=2)
                L.do(a.activation(EGC, s[:, :, 0], ACT.Exp))
                L.do(a.activation(EGL, s[:, :, 1], ACT.Exp), "v_exp")

                for n in range(5):
                    if n:
                        L.done(J(f"gs{n - 1}"))
                    s = L.full(J(f"grow{n}"))
                    L.do(a.activation(EG, s.rearrange("p (m i) -> p m i", m=8), ACT.Exp), "eg_ready")
                    L.need("dm_in")
                    L.do(a.activation(DM, DM, ACT.Exp), "dm_exp")
                    for v in range(1, LEV):
                        j = J(f"W{n}_{v}")
                        copy(Wb, L.full(j).rearrange("p (m i) -> p m i", m=8), j)
                    s = L.full(J(f"uw{n}"))
                    copy(u_b, s[:, 0:512].rearrange("p (m i) -> p m i", m=8))
                    copy(wT_b, s[:, 512:1024].rearrange("p (m i) -> p m i", m=4), J(f"uw{n}"))
                L.done(J("gs4"))

                def upper_gates(n):
                    for d in range(2):
                        L.do(a.activation(lp[0][:, d], lf[:, chunk(d, n), d * 256:(d + 1) * 256], ACT.Copy),
                             "lp_hi" if d else None)

                upper_gates(0)
                for n in range(5):
                    if n:
                        L.done(J(f"hs{n - 1}"))
                    for d in range(2):
                        L.do(a.activation(KK[:, d], lf[:, chunk(d, n), d * 256:(d + 1) * 256], ACT.Exp),
                             "kk_exp" if d else None)
                    s = L.full(J(f"hk{n}"))
                    copy(KTt, s[:, 0:512].rearrange("p (m i) -> p m i", m=4))
                    L.free(a.activation(RV, s[:, 512:1024].rearrange("p (m i) -> p m i", m=2), ACT.Exp), J(f"hk{n}"))
                    for x in range(4):
                        if x >= 2:
                            L.done(J(f"P{n}_{x - 2}_1"))
                        j = J(f"E{n}_{x}")
                        L.free(a.activation(Eb[x % 2], L.full(j).rearrange("p (m i) -> p m i", m=8), ACT.Exp), j)
                    if n < 4:
                        upper_gates(n + 1)
                L.done(J("hs4"))
                L.do(a.activation(o2[0][:, 0:4, :], hT[:, 0:4, :], ACT.Copy), "oa_hi")
                for t in range(4):
                    if t >= 2:
                        L.need("o_ready")
                    j = J(f"rs{t}")
                    L.free(a.activation(orb[t % 2], L.full(j)[:, 0:NT], ACT.Ln, scale=1.0 / HD, bias=eps[:, 0:1]), j)
                    L.do(a.activation(orb[t % 2], orb[t % 2], ACT.Exp, scale=-0.5), "r_ready")
                for t in range(4):
                    if t >= 2:
                        L.need("o_ready")
                    L.do(a.activation(o2[0][:, 4 + t, :], hT[:, 4 + t, :], ACT.Copy), "om_hi")
                for what in OUT_PIECES:
                    upper(l, what)

                def norm(i):
                    L.done(J(f"mean{i}"))
                    L.do(a.activation(hT[:, :, :], xT[:, :, :], ACT.Square), "sq_ready")
                    j = J(f"var{i}")
                    L.free(a.activation(rstd, L.full(j)[:, 0:NT], ACT.Ln, bias=eps[:, 0:1]), j)
                    L.do(a.activation(rstd, rstd, ACT.Exp, scale=-0.5), "rstd_ready")

                norm(1)
                upper_h(l, 24, 32, True)
                if l % 2:
                    L.need("v_in")
                    L.do(a.activation(tq[:, 0], tq[:, 0], ACT.Exp), "v_exp")
                    for e in range(NE):
                        j = J(f"cb{e}")
                        copy(combB[:, e, :], L.full(j)[:, 0:NT], j)
                base = PS_BASE[l]

                sbase = SPLIT_BASE[l]

                def slab(i):
                    for j, (bank, k) in enumerate(((1, -2), (3, -2), (3, 0))):
                        act.wait_ge(w_full[j], i * 64 + 64 * (WP_BASE[l][j] + 1))
                        a.activation(wpiece(j), wpiece(j), ACT.Copy, scale=WS).then_inc(sg["w_scaled"], 1)
                        act.wait_ge(sg["w_scaled"], i * 3 + (3 * A_BASE[l] // 2 + j + 1))
                        act.wait_ge(ps_full[bank], i * 3 + (base[bank] + k))
                        a.activation(parts(SPLIT_FFN[j], KT, 256)[0], wpiece(j), ACT.Copy).then_inc(sg["w_hi"], 1)
                    for t in range(2):
                        act.wait_ge(ps_full[t], i * 3 + (base[t] + 1))
                        a.activation(gbuf[:, t], ps[:, t, 0:NT], ACT.Silu, scale=IWS).then_inc(ps_free[t], 1)
                    for t in range(2):
                        act.wait_ge(ps_free[2 + t], i * 3 + (base[2 + t] + 1))
                        a.activation(a2[0][:, t], gbuf[:, t], ACT.Copy).then_inc(sg["a_hi"], 1)
                    act.wait_ge(sg["a_lo"], i * 2 + (A_BASE[l] + 2))

                if l % 2 == 0:
                    with act.Fori(0, SLABS[0]) as s:
                        slab(s)
                else:
                    with act.Fori(0, NE) as e:
                        with act.Fori(0, ES) as s:
                            slab(e * ES + s)
                L.made["w_hi"] = sbase + 3 * SLABS[l]
                norm(2)
            for t in range(TT):
                copy(xin[:, t, :], L.full(f"yt{t}"), f"yt{t}")

        def route(L, v_, tt, ts, J):
            s = L.full(J("router"))[:, 0:40].rearrange("p (t e) -> p t e", t=TT)
            ts(lg, s, IWS, ALU.mult, job=J("router"))
            tt(lg, lg, brr[:, :].unsqueeze(1).broadcast_to([P, TT, NE]), ALU.add)
            for t in range(TT):
                L.do(v_.max(top[:, t], lg[:, t]))
            tt(tq[:, 0], top[:, :, 1], top[:, :, 0], ALU.subtract, to="v_in")
            le = lg.unsqueeze(3).broadcast_to([P, TT, NE, NE])
            lo = lg.unsqueeze(2).broadcast_to([P, TT, NE, NE])
            tt(ggt, lo, le, ALU.is_gt)
            tt(geq, lo, le, ALU.is_equal)
            tt(geq, geq, tie.rearrange("p (a b) -> p a b", a=NE).unsqueeze(1).broadcast_to([P, TT, NE, NE]), ALU.mult)
            tt(ggt, ggt, geq, ALU.add)
            L.do(v_.tensor_reduce(comb, ggt, AX_X, ALU.add))
            ts(first, comb, 0.0, ALU.is_equal)
            ts(comb, comb, 1.0, ALU.is_equal)
            L.need("v_exp")
            ts(tq[:, 1], tq[:, 0], 1.0, ALU.add)
            L.do(v_.reciprocal(tq[:, 1], tq[:, 1]))
            tt(tq[:, 2], tq[:, 0], tq[:, 1], ALU.mult)
            tt(first, first, tq[:, 1].unsqueeze(2).broadcast_to([P, TT, NE]), ALU.mult)
            tt(comb, comb, tq[:, 2].unsqueeze(2).broadcast_to([P, TT, NE]), ALU.mult)
            tt(comb, comb, first, ALU.add, to="comb_ready")

        @block.vector
        def _(dve):
            L = Lane(dve, "dve_chain")
            v_ = nc.vector

            def tt(o, x, y, op, to=None, job=None):
                ins = v_.tensor_tensor(o, x, y, op)
                L.free(ins, job) if job else L.do(ins, to)

            def ts(o, x, s1, op0, s2=None, op1=ALU.bypass, to=None, job=None):
                ins = v_.tensor_scalar(o, x, s1, s2, op0, op1)
                L.free(ins, job) if job else L.do(ins, to)

            def stt(o, x, s, y, op0, op1, to=None, job=None):
                ins = v_.scalar_tensor_tensor(out=o, in0=x, scalar=s, in1=y, op0=op0, op1=op1)
                L.free(ins, job) if job else L.do(ins, to)

            L.do(v_.memset(eps[:, 0:1], 1e-5))
            L.do(v_.memset(eps[:, 1:2], 1e-6))
            dve.wait_ge(sg["tab_in"], 16 * (1 + PAR_DMAS))
            tt(lbt[:, :], lbrow[:, 0], lbrow[:, 1], ALU.max)
            tt(lbrow[:, 0], lbrow[:, 0], lbt[:, :], ALU.subtract)
            tt(lbrow[:, 1], lbrow[:, 1], lbt[:, :], ALU.subtract, to="lb_in")
            L.need("lb_exp")
            tt(lbrow[:, 0], lbrow[:, 0], lbrow[:, 1], ALU.add)
            L.do(v_.reciprocal(lbt[:, :], lbrow[:, 0]))
            tt(lbt[:, :], lbt[:, :], lbrow[:, 1], ALU.mult)
            L.done("par")
            L.done(f"xt{TT - 1}")

            def modulate(l, shift, scale):
                for k in range(KT):
                    for g, a0, a1 in groups:
                        ts(htmp[:, a0:a1], xT[:, k, a0:a1], modT[:, l, scale + k, g:g + 1], ALU.mult,
                           modT[:, l, shift + k, g:g + 1], ALU.add)
                    L.need("hi_ready")
                    tt(h2[1][:, k, :], htmp, h2[0][:, k, :], ALU.subtract, to="h_ready")
                ts(xT[:, :, :], xT[:, :, :], ALPHA, ALU.mult)

            def norm(l, i):
                j = f"{l}.mean{i}"
                tt(xT[:, :, :], xT[:, :, :], L.full(j)[:, 0:NT].unsqueeze(1).broadcast_to([P, KT, NT]), ALU.subtract, job=j)
                L.need("rstd_ready")
                tt(xT[:, :, :], xT[:, :, :], rstd.unsqueeze(1).broadcast_to([P, KT, NT]), ALU.mult)
                for k in range(KT):
                    at = P + (l * 2 + i - 1) * KT + k
                    ts(xT[:, k, :], xT[:, k, :], par[:, at:at + 1], ALU.mult, par[:, 32 + at:33 + at], ALU.add,
                       to="xn_ready" if (l, i) == (DEPTH - 1, 2) else "x_ready")

            def mod_chunk(l, c):
                j = f"{l}.mt{c}"
                M = modT[:, l, 8 * c:8 * c + 8, :]
                s = L.full(j)[:, 0:16].rearrange("p (t g) -> p t g", g=2)
                b = par[:, 48 * l + 8 * c:48 * l + 8 * c + 8].unsqueeze(2).broadcast_to([P, 8, 2])
                tt(M, s, b, ALU.add, job=j)
                if c % 3 == 1:
                    ts(M, M, 1.0, ALU.add, to="mod_ready" if (l, c) == (0, 1) else None)
                if c % 3 == 2:
                    ts(M, M, IWS, ALU.mult)

            mod_chunk(0, 0)
            mod_chunk(0, 1)

            for l in range(DEPTH):
                J = lambda name: f"{l}.{name}"
                modulate(l, 0, 8)
                L.need("pad_zero")
                for t in range(6):
                    s = L.full(J(f"b{t}"))
                    ts(pad[:, t, 2:2 + LAT], s[:, 0:LAT], IWS, ALU.mult)
                    ts(pad[:, t, 4 + LAT:4 + NT], s[:, LAT:NT], IWS, ALU.mult, job=J(f"b{t}"))
                ts(ba[:, :, :], L.full(J("ba"))[:, 0:80].rearrange("p (t n) -> p t n", t=TT), IWS, ALU.mult, job=J("ba"))
                for t in range(6):
                    for w in range(CONV):
                        at = P + 64 + (l * CONV + w) * 6 + t
                        if w == 0:
                            ts(cv[:, t, :], pad[:, t, 0:CVW], par[:, at:at + 1], ALU.mult)
                        else:
                            stt(cv[:, t, :], pad[:, t, w:w + CVW], par[:, at:at + 1], cv[:, t, :], ALU.mult, ALU.add,
                                to="conv_done" if (t, w) == (5, CONV - 1) else None)
                dve.wait_ge(sg["rope_in"], 16 * (l + 1))
                for t in range(5):
                    s = L.full(J(f"rot{t}"))
                    tt(rtmp, s[:, 0:LAT], sinT, ALU.mult, job=J(f"rot{t}"))
                    tt(qk[:, t, 0:LAT], qk[:, t, 0:LAT], cosT, ALU.mult)
                    tt(qk[:, t, 0:LAT], qk[:, t, 0:LAT], rtmp, ALU.add, to="rope_ready")

                def scores(x):
                    n, t = units[x]
                    _, _, w, _, m0 = window(n)
                    sm, S = small[:, x % 3], a_s[x % 3][:, :, 0:w]
                    j = J(f"S{n}_{t}")
                    s = L.full(j).rearrange("p (f w) -> p f w", f=2)[:, :, 0:w]
                    if n == 4:
                        ts(S, s, ATT_SCALE, ALU.mult, job=j)
                    else:
                        stt(S, s, ATT_SCALE, am[:, m0:m0 + w].unsqueeze(1).broadcast_to([P, 2, w]), ALU.mult, ALU.add, job=j)
                    L.do(v_.tensor_reduce(sm[:, 0:2], S, AX_X, ALU.max))
                    snk = sink[:, l * 8 + t:l * 8 + t + 5:4]
                    tt(sm[:, 0:2], sm[:, 0:2], snk, ALU.max)
                    ts(sm[:, 2:4], sm[:, 0:2], -1.0, ALU.mult)
                    tt(sm[:, 6:8], snk, sm[:, 0:2], ALU.subtract, to="sm_in")

                def divide(x):
                    w = window(units[x][0])[2]
                    sm, S = small[:, x % 3], a_s[x % 3]
                    L.need("sm_exp")
                    tt(sm[:, 8:10], sm[:, 4:6], sm[:, 6:8], ALU.add)
                    L.do(v_.reciprocal(sm[:, 10:12], sm[:, 8:10]))
                    for f in range(2):
                        ts(S[:, f, 0:w], S[:, f, 0:w], sm[:, 10 + f:11 + f], ALU.mult, to="prob_ready" if f else None)

                scores(0)
                scores(1)
                divide(0)
                for x in range(len(units)):
                    if x + 2 < len(units):
                        scores(x + 2)
                    if x + 1 < len(units):
                        divide(x + 1)
                    if l == 0 and x % 2:
                        lm, i = mod_piece(2 * (x - 1))
                        mod_chunk(lm, i // 4)
                L.done(J("O4_3"))
                ts(lfd, lfd, 1.0, ALU.add)
                L.do(v_.reciprocal(lfd, lfd))
                if l:
                    lbb = lbt[:, :].unsqueeze(1).broadcast_to([P, TT, 512])
                    tmp = lf2.rearrange("p (t n) -> p t n", t=TT)
                    tt(tmp, lf, lbb, ALU.mult)
                    tt(lf, lf, tmp, ALU.subtract)
                    tt(lf, lf, lbb, ALU.add)
                ts(lf2, lfd, 1e-30, ALU.max, 2.0 ** -60, ALU.min)
                ts(lf2, lf2, 2.0 ** 60, ALU.mult)
                ts(lfd, lfd, 2.0 ** -60, ALU.max, to="f_in")
                zb = ba[:, :, 0:8].rearrange("p t (d h) -> p d t h", d=2)
                za = ba[:, :, 8:16].rearrange("p t (d h) -> p d t h", d=2)

                def by_head(v):
                    return v[:, l * 8:l * 8 + 8].rearrange("p (d h) -> p d h", d=2).unsqueeze(2).broadcast_to([P, 2, TT, 4])

                def four(v):
                    return v.rearrange("p d (t h) -> p d t h", t=TT)

                L.do(v_.tensor_copy(four(BETA), zb))
                tt(four(ZA), za, by_head(dtb), ALU.add)
                stt(SP, ZA, -1.0, ZA, ALU.mult, ALU.max, to="ab_in")
                L.need("f_ln")
                tt(lfd, lfd, lf2, ALU.add, to="lf_ready")
                L.need("ab_exp")
                ts(BETA, BETA, 1.0, ALU.add)
                L.do(v_.reciprocal(BETA, BETA))
                stt(ZA, ZA, 0.0, SP, ALU.max, ALU.add)
                tt(four(ZA), four(ZA), by_head(alog), ALU.mult)
                ts(LA, ZA, -1.0, ALU.mult, to="la_ready")
                for t in range(4):
                    L.need("l2_r")
                    stt(cv[:, t, :], cv[:, t, :], HD ** -0.5 if t < 2 else 1.0, rsb[t % 2], ALU.mult, ALU.mult, to="l2_ready")
                s = L.full(J("gate"))[:, 0:80].rearrange("p (d k n) -> p d k n", d=2, k=2)
                L.need("v_exp")
                L.free(v_.tensor_copy(GC, s[:, :, 0]), J("gate"))
                tt(BG, BETA, EGC, ALU.mult, to="g_ready")

                def update(S, slot, weight, job, n, tile):
                    for d in range(2):
                        cc = chunk(d, n) * P
                        tt(hT[:, tile:tile + 2, cc:cc + P], hT[:, tile:tile + 2, cc:cc + P],
                           slot[:, d * 256:d * 256 + 256].rearrange("p (r i) -> p r i", r=2), ALU.add)
                    if n == 3:
                        L.free(v_.memset(S[:, :, :], 0.0), job)
                        return
                    for f in range(2):
                        r0, r1 = f * HD, (f + 1) * HD
                        for x in range(4):
                            stt(S[r0:r1, x, r0:r1], S[r0:r1, x, r0:r1], weight(f, x)[r0:r1],
                                slot[r0:r1, 512 + x * HD:512 + (x + 1) * HD], ALU.mult, ALU.add,
                                job=job if (f, x) == (1, 3) else None)

                L.need("o_zero")
                for n in range(5):
                    s = L.full(J(f"grow{n}")).rearrange("p (m i) -> p m i", m=8)
                    L.need("eg_ready")
                    for d in range(2):
                        gg = gate_of(GC, d, chunk(d, n)).unsqueeze(3).broadcast_to([P, 2, 2, P])
                        tt(per_dir(DM, d), per_dir(s, d), gg, ALU.subtract, job=J(f"grow{n}") if d else None)
                    ts(DM, DM, 0.0, ALU.min, to="dm_in")
                    L.need("dm_exp")
                    for f in range(2):
                        tt(per_half(DM, f), per_half(DM, f), inc.unsqueeze(2).broadcast_to([P, 2, 2, P]), ALU.mult)
                    eight = lambda j: L.full(J(j)).rearrange("p (m i) -> p m i", m=8)
                    tt(LT, DM, eight(f"brow{n}"), ALU.mult, job=J(f"brow{n}"))
                    tt(LT, LT, eight(f"G{n}"), ALU.mult, job=J(f"G{n}"))
                    tt(AT, DM, eight(f"KQ{n}"), ALU.mult, job=J(f"KQ{n}"))
                    idb = ident.unsqueeze(1).broadcast_to([P, 8, P])
                    tt(T_, idb, eight(f"W{n}_0"), ALU.subtract, job=J(f"W{n}_0"))
                    tt(Tt, idb, CS[0], ALU.subtract, to="t_ready")
                    for v in range(1, LEV):
                        if v < LEV - 1:
                            tt(T_, T_, eight(f"T{n}__{v}"), ALU.subtract, job=J(f"T{n}__{v}"))
                        tt(Tt, Tt, eight(f"TT{n}_{v}"), ALU.subtract, job=J(f"TT{n}_{v}"))
                    L.done(J(f"uw{n}"))
                    s = L.full(J(f"vn{n}"))
                    tt(vnew, u_b, s[:, 0:512].rearrange("p (m i) -> p m i", m=8), ALU.subtract, job=J(f"vn{n}"))
                    update(SG, L.full(J(f"gs{n}")), lambda f, x: EG[:, f * 4 + x, last_row(x // 2):last_row(x // 2) + 1],
                           J(f"gs{n}"), n, 4)
                for n in range(5):
                    L.need("kk_exp")
                    ts(KK, KK, -1.0, ALU.mult, 1.0, ALU.add, to="kk_ready")

                    def weigh_q(x):
                        d, r = divmod(x, 2)
                        cc = chunk(d, n) * P
                        L.done(J(f"E{n}_{x}"))
                        q = qc[:, r, cc:cc + P]
                        tt(QE[x % 2], Eb[x % 2][:, 0:7, :], q.unsqueeze(1).broadcast_to([P, 7, P]), ALU.mult)
                        tt(QB[:, x], Eb[x % 2][:, 7, :], q, ALU.mult)
                        L.do(v_.tensor_copy(ebl[:, x:x + 1], Eb[x % 2][:, 7, last_row(d):last_row(d) + 1]), "qe_ready")

                    weigh_q(0)
                    for x in range(4):
                        if x < 3:
                            weigh_q(x + 1)
                        for f in range(2):
                            j = J(f"P{n}_{x}_{f}")
                            tt(PM, L.full(j).rearrange("p (m i) -> p m i", m=8), mk[:, x // 2], ALU.mult, job=j)
                            L.do(v_.tensor_reduce(AH[:, f * 4 + x], PM.rearrange("p m i -> p i m"), AX_X, ALU.add),
                                 "ah_ready" if (x, f) == (3, 1) else None)
                    update(SH, L.full(J(f"hs{n}")), lambda f, x: ebl[:, x:x + 1], J(f"hs{n}"), n, 6)
                for t in range(4):
                    L.need("r_ready")
                    at = 2 * P + (t // 2) * 2 + l
                    stt(hT[:, 4 + t, :], hT[:, 4 + t, :], par[:, at:at + 1], orb[t % 2], ALU.mult, ALU.mult)
                    tt(hT[:, 4 + t, :], hT[:, 4 + t, :], gbc[:, t, :], ALU.mult, to="o_ready")
                for t in range(4):
                    L.need("om_hi")
                    tt(o2[1][:, 4 + t, :], hT[:, 4 + t, :], o2[0][:, 4 + t, :], ALU.subtract, to="om_lo")
                for m in range(KT):
                    s = L.full(J(f"wo{m}"))
                    for g, a0, a1 in groups:
                        stt(xT[:, m, a0:a1], s[:, a0:a1], modT[:, l, 16 + m, g:g + 1], xT[:, m, a0:a1], ALU.mult, ALU.add,
                            job=J(f"wo{m}") if g else None)
                norm(l, 1)
                modulate(l, 24, 32)
                L.do(v_.memset(yacc, 0.0))
                if l % 2:
                    route(L, v_, tt, ts, J)
                base = PS_BASE[l]

                def slab(i):
                    for t in range(2):
                        dve.wait_ge(ps_full[2 + t], i * 3 + (base[2 + t] + 1))
                        if l % 2:
                            dve.wait_ge(sg["g_comb"], i * 2 + (t + 1))
                        else:
                            dve.wait_ge(ps_free[t], i * 3 + (base[t] + 1))
                        v_.scalar_tensor_tensor(out=gbuf[:, t], in0=ps[:, 2 + t, 0:NT], scalar=IWS, in1=gbuf[:, t],
                                                op0=ALU.mult, op1=ALU.mult).then_inc(ps_free[2 + t], 1)
                    for m in range(KT):
                        b = m % 4
                        dve.wait_ge(ps_full[b], i * 3 + (base[b] + 2 + m // 4))
                        v_.tensor_tensor(yacc[:, m], yacc[:, m], ps[:, b, 0:NT], ALU.add).then_inc(ps_free[b], 1)

                if l % 2 == 0:
                    with dve.Fori(0, SLABS[0]) as s:
                        slab(s)
                else:
                    with dve.Fori(0, NE) as e:
                        with dve.Fori(0, ES) as s:
                            slab(e * ES + s)
                for b in range(4):
                    dve.wait_ge(ps_free[b], base[b] + 3 * SLABS[l])
                for m in range(KT):
                    for g, a0, a1 in groups:
                        stt(xT[:, m, a0:a1], yacc[:, m, a0:a1], modT[:, l, 40 + m, g:g + 1], xT[:, m, a0:a1], ALU.mult, ALU.add,
                            to="z_ready" if (m, g) == (KT - 1, 1) else None)
                norm(l, 2)

        @block.tensor
        def _(pe):
            L = Lane(pe, None)
            mm_, tr_ = nc.tensor.matmul, nc.tensor.transpose

            def open_(job):
                slot, turn = PS[job]
                if turn:
                    pe.wait_ge(ps_free[slot], turn)
                return ps[:, slot]

            def close(ins, job):
                ins.then_inc(ps_full[PS[job][0]], 1)

            def piece(name):
                slot, turn = WP[name]
                pe.wait_ge(w_full[slot], 64 * (turn + 1))
                return wpiece(slot)

            def mm(o, w, x, first=True, last=True):
                return mm_(o, w, x, start=first, stop=last, skip_group_check=True)

            def wide(s, w, x, first, last):
                mm(s[:, 0:LAT], w, x[:, 0:LAT], first, last)
                return mm(s[:, LAT:NT], w, x[:, LAT:NT], first, last)

            def split_piece(l, what):
                pe.wait_ge(sg["w_lo"], SPLIT[f"{l}.{what}"] + 1)
                return split_parts(what)

            def three(s, w, x, first, last):
                wide(s, w[0], x[0], first, False)
                wide(s, w[0], x[1], False, False)
                return wide(s, w[1], x[0], False, last)

            def project(l, what, job, lo, x, arriving=False):
                w = split_piece(l, what)
                s = open_(job)
                for k in range(KT):
                    if arriving:
                        L.need("h_ready")
                    ins = three(s, [v[:, k, lo:lo + P] for v in w], [v[:, k] for v in x], k == 0, k == KT - 1)
                close(ins, job)

            cvec = siluc[:, :].rearrange("p (g k) -> p k g", g=2)

            def mod_piece_job(l, i):
                w = piece(f"{l}.mod{i}")
                s = open_(f"{l}.mp{i}")
                for k in range(KT):
                    ins = mm(s[0:2, 0:256], cvec[:, k], w[:, k], k == 0, k == KT - 1)
                close(ins, f"{l}.mp{i}")

            def mod_turn(l, c):
                s = open_(f"{l}.mt{c}")
                L.done(f"{l}.mp{4 * c + 3}")
                for k in range(KT):
                    ins = tr_(s[:, 2 * k:2 * k + 2], modrow[0:2, k * P:(k + 1) * P], ident[0:2, 0:2])
                close(ins, f"{l}.mt{c}")

            pe.wait_ge(sg["tab_in"], 16 * (1 + PAR_DMAS))
            pe.wait_ge(sg["x_in"], 16 * TT)
            for t in range(TT):
                s = open_(f"xt{t}")
                for k in range(KT):
                    ins = tr_(s[:, k * P:(k + 1) * P], xin[:, t, k * P:(k + 1) * P], ident)
                close(ins, f"xt{t}")
            s = open_("par")
            for k in range(3):
                ins = tr_(s[:, k * P:(k + 1) * P], rows[:, k, :], ident)
            close(ins, "par")
            L.need("siluc_ready")
            for i in range(8):
                mod_piece_job(0, i)
                if i % 4 == 3:
                    mod_turn(0, i // 4)

            for l in range(DEPTH):
                J = lambda name: f"{l}.{name}"
                for t in range(4):
                    project(l, f"qa{t // 2}", J(f"q{t}"), (t % 2) * P, h2, t == 0)
                project(l, "kv", J("ka"), 0, h2)
                w = split_piece(l, "kv")

                def tokens(job, w, cols, tiles):
                    s = open_(job)
                    lo, hi = cols
                    n = hi - lo
                    for i, t in enumerate(tiles):
                        for k in range(KT):
                            for a_, b_ in ((0, 0), (0, 1), (1, 0)):
                                ins = mm(s[:, i * n:(i + 1) * n], h2[a_][:, k, t * P:(t + 1) * P], w[b_][:, k, lo:hi],
                                         k + a_ + b_ == 0, (k, a_) == (KT - 1, 1))
                    close(ins, job)

                tokens(J("va"), w, (P, 256), range(TT))
                for t in range(6):
                    project(l, f"b{t // 2}", J(f"b{t}"), (t % 2) * P, h2)
                for t in range(2):
                    project(l, "gb", J(f"gb{t}"), t * P, h2)
                tokens(J("ba"), split_piece(l, "ba"), (0, 16), range(TT))
                for p_ in ("f0", "f1", "i"):
                    w = split_piece(l, p_)
                    tokens(J(p_ + "a"), w, (0, 256), range(4))
                    tokens(J(p_ + "b"), w, (0, 256), range(4, 5))
                for p_ in ("qc", "gc"):
                    for t in range(2):
                        project(l, p_, J(f"{p_}{t}"), t * P, h2)
                L.done(J("ka"))
                s = open_(J("kout"))
                close(tr_(s[:, 0:P], qk[:, 4, LAT:NT], ident), J("kout"))
                pe.wait_ge(sg["cache_in"], 32 * (l + 1))
                s = open_(J("ckt"))
                close(tr_(s[:, 0:P], cachek[:, :], ident), J("ckt"))
                for t in range(5):
                    s = open_(J(f"rot{t}"))
                    close(mm(s[:, 0:LAT], rot, qk[:, t, 0:LAT]), J(f"rot{t}"))
                L.need("rope_ready", 5)
                L.done(J("ckt"))
                L.done(J("va"))

                def score(x):
                    n, t = units[x]
                    cache_at, band_at, w, tok, _ = window(n)
                    s = open_(J(f"S{n}_{t}"))
                    for f in range(2):
                        r0, r1 = f * HD, (f + 1) * HD
                        q = qk[r0:r1, t, n * P:(n + 1) * P]
                        band = w - (P if cache_at is not None else 0)
                        ins = mm(s[:, f * 512 + band_at:f * 512 + band_at + band], q, qk[r0:r1, 4, tok:tok + band])
                        if cache_at is not None:
                            ins = mm(s[:, f * 512 + cache_at:f * 512 + cache_at + P], q, cachekT[r0:r1, :])
                    close(ins, J(f"S{n}_{t}"))

                def output(x):
                    n, t = units[x]
                    cache_at, band_at, w, tok, _ = window(n)
                    s = open_(J(f"O{n}_{t}"))
                    L.done(J(f"T{n}_{t}"))
                    for f in range(2):
                        for b in range(w // P):
                            if cache_at is not None and b * P == cache_at:
                                vals = cachev[:, f * HD:(f + 1) * HD]
                            else:
                                vals = va[:, (tok + b * P - band_at) // P, f * HD:(f + 1) * HD]
                            ins = mm(s[f * HD:(f + 1) * HD, 0:P], vals, a_pT[x % 2][:, f, b * P:(b + 1) * P],
                                     b == 0, b == w // P - 1)
                    close(ins, J(f"O{n}_{t}"))

                score(0)
                score(1)
                for x, (n, t) in enumerate(units):
                    if x + 2 < len(units):
                        score(x + 2)
                    w = window(n)[2]
                    L.need("prob_ready")
                    s = open_(J(f"T{n}_{t}"))
                    for f in range(2):
                        for b in range(w // P):
                            ins = tr_(s[:, f * 512 + b * P:f * 512 + (b + 1) * P], a_s[x % 3][:, f, b * P:(b + 1) * P], ident)
                    close(ins, J(f"T{n}_{t}"))
                    if l == 0:
                        for i in mod_pieces(x):
                            mod_piece_job(*mod_piece(i))
                    if x:
                        output(x - 1)
                    if l == 0 and x % 2:
                        lm, i = mod_piece(2 * (x - 1))
                        mod_turn(lm, i // 4)
                output(len(units) - 1)

                L.need("l2_sq")
                for t in range(4):
                    s = open_(J(f"l2{t}"))
                    mm(s[:, 0:512], blk, sqb[:, t, 0:512])
                    close(mm(s[:, 512:CVW], blk, sqb[:, t, 512:CVW]), J(f"l2{t}"))
                L.need("l2_ready", 4)
                for t in range(TT):
                    s = open_(J(f"kv{t}"))
                    cc = cv_col(t)
                    for i in range(4):
                        ins = tr_(s[:, i * P:(i + 1) * P], cv[:, 2 + i, cc:cc + P], ident)
                    close(ins, J(f"kv{t}"))
                L.need("la_ready")
                s = open_(J("gate"))
                for d in range(2):
                    mm(s[:, d * 40:d * 40 + 20], inc[:, d], LA[:, d])
                    ins = mm(s[:, d * 40 + 20:d * 40 + 40], rev[:, d], LA[:, d])
                close(ins, J("gate"))
                if l == 0:
                    pe.wait_ge(sg["state_in"], 64)
                else:
                    pe.wait_ge(sg["state_in"], 128)

                problems = [(f, d, r) for f in range(2) for d in range(2) for r in range(2)]
                L.done(J("gate"))
                for n in range(5):
                    def gate_row(v, d, r, f):
                        at = 4 * chunk(d, n) + 2 * r + f
                        return v[:, d, at:at + 1].broadcast_to([P, P])

                    def at(m):
                        return slice(m * P, (m + 1) * P)

                    s = open_(J(f"grow{n}"))
                    for m, (f, d, r) in enumerate(problems):
                        ins = mm(s[:, at(m)], gate_row(LA, d, r, f), inc[:, d])
                    close(ins, J(f"grow{n}"))
                    s = open_(J(f"brow{n}"))
                    for m, (f, d, r) in enumerate(problems):
                        ins = mm(s[:, at(m)], gate_row(BETA, d, r, f), ident)
                    close(ins, J(f"brow{n}"))
                    for job, first_tile in ((J(f"G{n}"), 2), (J(f"KQ{n}"), 0)):
                        s = open_(job)
                        for m, (f, d, r) in enumerate(problems):
                            cc = cv_col(chunk(d, n))
                            r0, r1 = f * HD, (f + 1) * HD
                            ins = mm(s[:, at(m)], cv[r0:r1, 2 + r, cc:cc + P], cv[r0:r1, first_tile + r, cc:cc + P])
                        close(ins, job)
                    L.need("cs_ready")
                    s = open_(J(f"W{n}_0"))
                    for m in range(8):
                        ins = mm(s[:, at(m)], CS[0][:, m], ident)
                    close(ins, J(f"W{n}_0"))
                    for v in range(1, LEV):
                        L.need("cs_ready")
                        if v == 1:
                            L.need("t_ready")
                        else:
                            L.done(J(f"TT{n}_{v - 1}"))
                        s = open_(J(f"W{n}_{v}"))
                        for m in range(8):
                            ins = mm(s[:, at(m)], CS[v % 2][:, m], T_[:, m])
                        close(ins, J(f"W{n}_{v}"))
                        L.done(J(f"W{n}_{v}"))
                        if v < LEV - 1:
                            s = open_(J(f"T{n}__{v}"))
                            for m in range(8):
                                ins = mm(s[:, at(m)], Tt[:, m], Wb[:, m])
                            close(ins, J(f"T{n}__{v}"))
                        s = open_(J(f"TT{n}_{v}"))
                        for m in range(8):
                            ins = mm(s[:, at(m)], Wb[:, m], Tt[:, m])
                        close(ins, J(f"TT{n}_{v}"))
                    L.need("vk_ready")
                    L.done(J(f"TT{n}_{LEV - 1}"))
                    s = open_(J(f"uw{n}"))
                    for m, (f, d, r) in enumerate(problems):
                        mm(s[:, m * HD:(m + 1) * HD], Tt[:, m], vb[:, m])
                        x = 2 * d + r
                        ins = mm(s[f * HD:(f + 1) * HD, 512 + x * P:512 + (x + 1) * P], kbg[:, m], Tt[:, m])
                    close(ins, J(f"uw{n}"))
                    L.done(J(f"uw{n}"))
                    s = open_(J(f"vn{n}"))
                    if n:
                        L.done(J(f"gs{n - 1}"))
                    for x in range(4):
                        for f in range(2):
                            m = f * 4 + x
                            ins = mm(s[:, m * HD:(m + 1) * HD], wT_b[:, x], SG[:, x, f * HD:(f + 1) * HD])
                    close(ins, J(f"vn{n}"))
                    L.done(J(f"vn{n}"))
                    L.done(J(f"KQ{n}"))
                    s = open_(J(f"gs{n}"))
                    for x in range(4):
                        mm(s[:, at(x)], SG[:, x], qg[:, x], True, False)
                        for f in range(2):
                            mm(s[f * HD:(f + 1) * HD, at(x)], vnew[:, f * 4 + x], AT[:, f * 4 + x], False, True)
                    for x in range(4):
                        for f in range(2):
                            ins = mm(s[f * HD:(f + 1) * HD, 512 + x * HD:512 + (x + 1) * HD], kd[:, f * 4 + x],
                                     vnew[:, f * 4 + x])
                    close(ins, J(f"gs{n}"))

                for n in range(5):
                    L.need("kk_ready")
                    L.need("lp_lo")
                    if (l, n) == (0, 0):
                        L.need("hg_ready")
                    s = open_(J(f"hk{n}"))
                    for x in range(4):
                        tr_(s[:, x * P:(x + 1) * P], KK[:, x // 2, (x % 2) * P:(x % 2 + 1) * P], ident)
                    for d in range(2):
                        for i in range(2):
                            ins = mm(s[:, 512 + d * 256:512 + (d + 1) * 256], rev16[:, d], lp[i][:, d], i == 0, i == 1)
                    close(ins, J(f"hk{n}"))

                    def exponents(x):
                        d, r = divmod(x, 2)
                        s = open_(J(f"E{n}_{x}"))
                        for b in range(2):
                            for i in range(2):
                                ins = mm(s[:, b * 512:(b + 1) * 512], lp[i][:, d, r * P:(r + 1) * P],
                                         hg16[:, d, 4 * b:4 * b + 4], i == 0, i == 1)
                        close(ins, J(f"E{n}_{x}"))

                    exponents(0)
                    for x in range(4):
                        if x < 3:
                            exponents(x + 1)
                        d, r = divmod(x, 2)
                        L.need("qe_ready")
                        L.need("ke_ready")
                        for f in range(2):
                            r0, r1 = f * HD, (f + 1) * HD
                            s = open_(J(f"P{n}_{x}_{f}"))
                            for v in range(LEV):
                                mm(s[:, v * P:(v + 1) * P], KE[x % 2][r0:r1, v], QE[x % 2][r0:r1, v])
                            cc = chunk(d, n) * P
                            ins = mm(s[:, 7 * P:8 * P], KTt[r0:r1, x], qc[r0:r1, r, cc:cc + P])
                            close(ins, J(f"P{n}_{x}_{f}"))
                    L.need("ah_ready")
                    L.need("kd_ready")
                    if n:
                        L.done(J(f"hs{n - 1}"))
                    s = open_(J(f"hs{n}"))
                    for x in range(4):
                        d, r = divmod(x, 2)
                        mm(s[:, x * P:(x + 1) * P], SH[:, x], QB[:, x], True, False)
                        for f in range(2):
                            h = 2 * r + f
                            mm(s[f * HD:(f + 1) * HD, x * P:(x + 1) * P], iv[:, chunk(d, n), h * HD:(h + 1) * HD],
                               AH[:, f * 4 + x], False, True)
                    for x in range(4):
                        d, r = divmod(x, 2)
                        for f in range(2):
                            h = 2 * r + f
                            ins = mm(s[f * HD:(f + 1) * HD, 512 + x * HD:512 + (x + 1) * HD],
                                     KD[:, d, h * HD:(h + 1) * HD], iv[:, chunk(d, n), h * HD:(h + 1) * HD])
                    close(ins, J(f"hs{n}"))

                L.need("o_sq")
                for t in range(4):
                    s = open_(J(f"rs{t}"))
                    close(wide(s, blk, osq[:, t], True, True), J(f"rs{t}"))
                L.need("oa_lo")
                L.need("om_lo", 4)
                for m in range(KT):
                    project(l, f"wo{m // 2}", J(f"wo{m}"), (m % 2) * P, o2)

                def over_features(job, x):
                    s = open_(job)
                    for k in range(KT):
                        ins = wide(s, mean, x[:, k], k == 0, k == KT - 1)
                    close(ins, job)

                L.done(J(f"wo{KT - 1}"))
                over_features(J("mean1"), xT)
                L.need("sq_ready")
                over_features(J("var1"), hT)
                L.need("h_ready", KT)
                if l % 2:
                    L.need("wr_ready")
                    s = open_(J("router"))
                    for t in range(TT):
                        for k in range(KT):
                            for a_, b_ in ((0, 0), (0, 1), (1, 0)):
                                ins = mm(s[:, t * NE:(t + 1) * NE], h2[a_][:, k, t * P:(t + 1) * P], wr2[b_][:, k],
                                         k + a_ + b_ == 0, (k, a_) == (KT - 1, 1))
                    close(ins, J("router"))
                    L.need("comb_ready")
                    for e in range(NE):
                        s = open_(J(f"cb{e}"))
                        for t in range(TT):
                            ins = mm(s[:, t * P:(t + 1) * P], comb[:, t, e:e + 1].broadcast_to([P, P]), ident)
                        close(ins, J(f"cb{e}"))
                base, sbase = PS_BASE[l], SPLIT_BASE[l]

                def slab(i):
                    for j in range(4):
                        if j % 2 == 0:
                            pe.wait_ge(sg["w_lo"], i * 3 + (sbase + j // 2 + 1))
                        pe.wait_ge(ps_free[j], i * 3 + base[j])
                        w = parts(SPLIT_FFN[j // 2], KT, 256)
                        for k in range(KT):
                            ins = three(ps[:, j], [v[:, k, (j % 2) * P:(j % 2 + 1) * P] for v in w], [v[:, k] for v in h2],
                                        k == 0, k == KT - 1)
                        ins.then_inc(ps_full[j], 1)
                    pe.wait_ge(sg["w_lo"], i * 3 + (sbase + 3))
                    w2 = parts(SPLIT_FFN[2], 2, 1024)

                    def down(m, t):
                        return three(ps[:, m % 4], [v[:, t, m * P:(m + 1) * P] for v in w2], [v[:, t] for v in a2],
                                     t == 0, t == 1)

                    pe.wait_ge(sg["a_lo"], i * 2 + (A_BASE[l] + 1))
                    for m in range(3):
                        pe.wait_ge(ps_free[m], i * 3 + (base[m] + 1))
                        down(m, 0)
                    pe.wait_ge(sg["a_lo"], i * 2 + (A_BASE[l] + 2))
                    for m in range(KT):
                        b = m % 4
                        if m >= 3:
                            pe.wait_ge(ps_free[b], i * 3 + (base[b] + 1 + m // 4))
                            down(m, 0)
                        down(m, 1).then_inc(ps_full[b], 1)

                if l % 2 == 0:
                    with pe.Fori(0, SLABS[0]) as s:
                        slab(s)
                else:
                    with pe.Fori(0, NE) as e:
                        with pe.Fori(0, ES) as s:
                            slab(e * ES + s)
                L.need("z_ready")
                over_features(J("mean2"), xT)
                L.need("sq_ready")
                over_features(J("var2"), hT)
            L.need("xn_ready", KT)
            for t in range(TT):
                s = open_(f"yt{t}")
                for k in range(KT):
                    ins = tr_(s[:, k * P:(k + 1) * P], xT[:, k, t * P:(t + 1) * P], ident)
                close(ins, f"yt{t}")


PAR_DMAS = 16
_INS = ["x_prompt", "x_sample", "cache_k", "cache_v", "state_gdn", "state_hgrn", "c", "c_ctx", "w_mod", "b_mod", "w_in",
        "conv_w", "attn_sink", "gdn_a_log", "gdn_dt_bias", "gdn_norm_w", "hgrn_lb", "hgrn_norm_w", "w_out", "ln_g", "ln_b",
        "ffn_w1", "ffn_w3", "ffn_w2", "moe_router", "moe_router_b", "moe_w1", "moe_w3", "moe_w2"]
_OUTS = [(1, CTX, D), (1, LAT, D), (1, DEPTH, CTX, 2, HD), (1, DEPTH, CTX, 2, HD), (1, DEPTH, 2, 4, HD, HD),
         (1, DEPTH, 2, 4, HD, HD)]


def kernel(**inputs):
    import concourse.bacc as bacc
    from concourse.bass_utils import run_bass_kernel_spmd

    nc = bacc.Bacc("TRN2", target_bir_lowering=False, num_devices=1)
    arrays, args = {}, []
    for name in _INS + ["table"]:
        a = np.ascontiguousarray(constant_table() if name == "table" else inputs[name])
        arrays[f"in_{name}"] = a
        args.append(nc.dram_tensor(f"in_{name}", a.shape, mybir.dt.from_np(a.dtype), kind="ExternalInput").ap())
    for i, shape in enumerate(_OUTS):
        args.append(nc.dram_tensor(f"out_{i}", shape, F32, kind="ExternalOutput").ap())
    backbone_kernel(nc, *args)
    r = run_bass_kernel_spmd(nc, [arrays], core_ids=[0])
    return tuple(r.results[0][f"out_{i}"] for i in range(len(_OUTS)))
```
